# Optimizing a Trainium2 kernel written in Bass

```python
import math
import jax, jax.numpy as jnp
from jax import lax
import numpy as np

D_MODEL = 1024
BATCH = 1
SEQ = 512
DEPTH = 1

MEM_LEN = 256
N_BRANCH = 3
CONV_WIDTH = D_MODEL // 2
CONV_TAPS = 3
SSM_WIDTH = D_MODEL // 2
SSM_GROUP = 16
SSM_GROUPS = SSM_WIDTH // SSM_GROUP
SSM_STATE = 64
XATTN_HEADS = 4
XATTN_HEAD_DIM = 128
XATTN_WIDTH = XATTN_HEADS * XATTN_HEAD_DIM
D_FF = 4 * D_MODEL
GATE_COLS = N_BRANCH * D_MODEL
IN_COLS = GATE_COLS + 3 * CONV_WIDTH + SSM_WIDTH + XATTN_WIDTH
ALPHA = (2.0 * DEPTH) ** 0.25
BETA = (8.0 * DEPTH) ** -0.25
LN_EPS = 1e-5
DT_MIN = 1e-3
DT_MAX = 1e-1

kernel_name = "hybrid_gated_conv_s5_xattn_deepnorm"

def layer_norm(x, g, b):
    xf = x.astype(jnp.float32)
    mu = jnp.mean(xf, axis=-1, keepdims=True)
    var = jnp.mean(jnp.square(xf - mu), axis=-1, keepdims=True)
    y = (xf - mu) * lax.rsqrt(var + LN_EPS) * g.astype(jnp.float32) + b.astype(jnp.float32)
    return y.astype(x.dtype)

def causal_dwconv(z, w):
    s = z.shape[1]
    zp = jnp.pad(z, ((0, 0), (CONV_TAPS - 1, 0), (0, 0)))
    y = w[0] * zp[:, 0:s]
    for k in range(1, CONV_TAPS):
        y = y + w[k] * zp[:, k:k + s]
    return y

def _complex_affine_combine(e1, e2):
    a1r, a1i, b1r, b1i = e1
    a2r, a2i, b2r, b2i = e2
    ar = a1r * a2r - a1i * a2i
    ai = a1r * a2i + a1i * a2r
    br = a2r * b1r - a2i * b1i + b2r
    bi = a2r * b1i + a2i * b1r + b2i
    return (ar, ai, br, bi)

def s5_mixer(u, lam_re, lam_im, log_dt, b_re, b_im, c_re, c_im, d_skip):
    bsz, s, _ = u.shape
    f32 = jnp.float32
    uf = u.astype(f32).reshape(bsz, s, SSM_GROUPS, SSM_GROUP)
    lr = lam_re.astype(f32)
    li = lam_im.astype(f32)
    dt = jnp.exp(log_dt.astype(f32))[:, None]
    mag = jnp.exp(lr * dt)
    abar_r = mag * jnp.cos(li * dt)
    abar_i = mag * jnp.sin(li * dt)
    den = lr * lr + li * li
    nr = abar_r - 1.0
    ni = abar_i
    kr = (nr * lr + ni * li) / den
    ki = (ni * lr - nr * li) / den
    br_ = b_re.astype(f32)
    bi_ = b_im.astype(f32)
    bbar_r = kr[..., None] * br_ - ki[..., None] * bi_
    bbar_i = kr[..., None] * bi_ + ki[..., None] * br_
    bu_r = jnp.einsum("bsgh,gph->bsgp", uf, bbar_r)
    bu_i = jnp.einsum("bsgh,gph->bsgp", uf, bbar_i)
    a_r = jnp.broadcast_to(abar_r, bu_r.shape)
    a_i = jnp.broadcast_to(abar_i, bu_r.shape)
    _, _, st_r, st_i = lax.associative_scan(_complex_affine_combine, (a_r, a_i, bu_r, bu_i), axis=1)
    y = (jnp.einsum("bsgp,ghp->bsgh", st_r, c_re.astype(f32))
         - jnp.einsum("bsgp,ghp->bsgh", st_i, c_im.astype(f32)))
    y = y.reshape(bsz, s, SSM_WIDTH) + d_skip.astype(f32) * uf.reshape(bsz, s, SSM_WIDTH)
    return y.astype(u.dtype)

def memory_cross_attention(q, mem, w_kv, w_xo):
    bsz, s, _ = q.shape
    kv = jnp.einsum("bmd,dn->bmn", mem, w_kv)
    k, v = jnp.split(kv, 2, axis=-1)
    qh = q.reshape(bsz, s, XATTN_HEADS, XATTN_HEAD_DIM)
    kh = k.reshape(bsz, -1, XATTN_HEADS, XATTN_HEAD_DIM)
    vh = v.reshape(bsz, -1, XATTN_HEADS, XATTN_HEAD_DIM)
    scores = jnp.einsum("bshd,bmhd->bhsm", qh, kh).astype(jnp.float32) * (XATTN_HEAD_DIM ** -0.5)
    probs = jax.nn.softmax(scores, axis=-1).astype(vh.dtype)
    o = jnp.einsum("bhsm,bmhd->bshd", probs, vh).reshape(bsz, s, XATTN_WIDTH)
    return jnp.einsum("bsc,cd->bsd", o, w_xo)

def setup_inputs(seed: int = 0) -> dict:
    key = jax.random.key(seed)
    ks = jax.random.split(key, 32)
    f32 = jnp.float32
    L, D = DEPTH, D_MODEL

    def nrm(k, shape, std):
        return jax.random.normal(k, shape, f32) * std

    x = jax.random.normal(ks[0], (BATCH, SEQ, D), f32)
    mem = jax.random.normal(ks[1], (BATCH, MEM_LEN, D), f32)
    w_in = nrm(ks[2], (L, D, IN_COLS), D ** -0.5)
    b_gate = nrm(ks[3], (L, GATE_COLS), 0.02)
    conv_w = nrm(ks[4], (L, CONV_TAPS, CONV_WIDTH), CONV_TAPS ** -0.5)
    w_conv_out = nrm(ks[5], (L, CONV_WIDTH, D), CONV_WIDTH ** -0.5)
    n_idx = jnp.arange(SSM_STATE, dtype=f32)
    ssm_lam_re = -0.5 + nrm(ks[6], (L, SSM_GROUPS, SSM_STATE), 0.01)
    ssm_lam_im = math.pi * n_idx + nrm(ks[7], (L, SSM_GROUPS, SSM_STATE), 0.01)
    ssm_log_dt = jax.random.uniform(ks[8], (L, SSM_GROUPS), f32, math.log(DT_MIN), math.log(DT_MAX))
    bstd = (2.0 * SSM_GROUP) ** -0.5
    ssm_b_re = nrm(ks[9], (L, SSM_GROUPS, SSM_STATE, SSM_GROUP), bstd)
    ssm_b_im = nrm(ks[10], (L, SSM_GROUPS, SSM_STATE, SSM_GROUP), bstd)
    cstd = (2.0 * SSM_STATE) ** -0.5
    ssm_c_re = nrm(ks[11], (L, SSM_GROUPS, SSM_GROUP, SSM_STATE), cstd)
    ssm_c_im = nrm(ks[12], (L, SSM_GROUPS, SSM_GROUP, SSM_STATE), cstd)
    ssm_d = nrm(ks[13], (L, SSM_WIDTH), 1.0)
    w_glu = nrm(ks[14], (L, SSM_WIDTH, 2 * D), SSM_WIDTH ** -0.5)
    w_k = nrm(ks[15], (L, D, XATTN_WIDTH), D ** -0.5)
    w_v = nrm(ks[16], (L, D, XATTN_WIDTH), BETA * D ** -0.5)
    w_kv = jnp.concatenate([w_k, w_v], axis=-1)
    w_xattn_out = nrm(ks[17], (L, XATTN_WIDTH, D), XATTN_WIDTH ** -0.5)
    w_out = nrm(ks[18], (L, D, D), BETA * D ** -0.5)
    ln1_g = 1.0 + nrm(ks[19], (L, D), 0.02)
    ln1_b = nrm(ks[20], (L, D), 0.02)
    w_up = nrm(ks[21], (L, D, D_FF), BETA * D ** -0.5)
    b_up = nrm(ks[22], (L, D_FF), 0.02)
    w_down = nrm(ks[23], (L, D_FF, D), BETA * D_FF ** -0.5)
    b_down = nrm(ks[24], (L, D), 0.02)
    ln2_g = 1.0 + nrm(ks[25], (L, D), 0.02)
    ln2_b = nrm(ks[26], (L, D), 0.02)
    return {"x": x, "mem": mem, "w_in": w_in, "b_gate": b_gate, "conv_w": conv_w,
            "w_conv_out": w_conv_out, "ssm_lam_re": ssm_lam_re, "ssm_lam_im": ssm_lam_im,
            "ssm_log_dt": ssm_log_dt, "ssm_b_re": ssm_b_re, "ssm_b_im": ssm_b_im,
            "ssm_c_re": ssm_c_re, "ssm_c_im": ssm_c_im, "ssm_d": ssm_d, "w_glu": w_glu,
            "w_kv": w_kv, "w_xattn_out": w_xattn_out, "w_out": w_out, "ln1_g": ln1_g,
            "ln1_b": ln1_b, "w_up": w_up, "b_up": b_up, "w_down": w_down, "b_down": b_down,
            "ln2_g": ln2_g, "ln2_b": ln2_b}

def reference(x, mem, w_in, b_gate, conv_w, w_conv_out, ssm_lam_re, ssm_lam_im, ssm_log_dt,
              ssm_b_re, ssm_b_im, ssm_c_re, ssm_c_im, ssm_d, w_glu, w_kv, w_xattn_out, w_out,
              ln1_g, ln1_b, w_up, b_up, w_down, b_down, ln2_g, ln2_b):
    bsz, s, d = x.shape
    splits = [GATE_COLS, GATE_COLS + 3 * CONV_WIDTH, GATE_COLS + 3 * CONV_WIDTH + SSM_WIDTH]
    for l in range(DEPTH):
        proj = jnp.einsum("bsd,dn->bsn", x, w_in[l])
        gate_pre, conv_in, u, q = jnp.split(proj, splits, axis=-1)
        gates = jax.nn.sigmoid(gate_pre + b_gate[l]).reshape(bsz, s, N_BRANCH, d)

        cb, cc, ch = jnp.split(conv_in, 3, axis=-1)
        y_a = jnp.einsum("bsc,cd->bsd", cb * causal_dwconv(cc * ch, conv_w[l]), w_conv_out[l])

        y_s = jax.nn.gelu(s5_mixer(u, ssm_lam_re[l], ssm_lam_im[l], ssm_log_dt[l], ssm_b_re[l],
                                   ssm_b_im[l], ssm_c_re[l], ssm_c_im[l], ssm_d[l]))
        glu_a, glu_b = jnp.split(jnp.einsum("bsc,cn->bsn", y_s, w_glu[l]), 2, axis=-1)
        y_b = glu_a * jax.nn.sigmoid(glu_b)

        y_c = memory_cross_attention(q, mem, w_kv[l], w_xattn_out[l])

        merged = gates[:, :, 0] * y_a + gates[:, :, 1] * y_b + gates[:, :, 2] * y_c
        x = layer_norm(ALPHA * x + jnp.einsum("bsd,de->bse", merged, w_out[l]), ln1_g[l], ln1_b[l])

        hdn = jnp.square(jax.nn.relu(jnp.einsum("bsd,df->bsf", x, w_up[l]) + b_up[l]))
        x = layer_norm(ALPHA * x + jnp.einsum("bsf,fd->bsd", hdn, w_down[l]) + b_down[l],
                       ln2_g[l], ln2_b[l])
    return x


_drawn_inputs = setup_inputs


def setup_inputs(seed=0):
    import zlib

    import numpy as np

    out = dict(_drawn_inputs(seed))
    spreads = {}
    factors = {'mem': 3.587,
     'b_gate': 8.0,
     'ssm_lam_re': 64.0,
     'ssm_lam_im': 64.0,
     'ssm_log_dt': 64.0,
     'ssm_b_re': 64.0,
     'ssm_b_im': 64.0,
     'ssm_c_re': 64.0,
     'ssm_c_im': 64.0,
     'w_kv': 3.24,
     'w_xattn_out': 3.472,
     'ln1_g': 7.688,
     'ln1_b': 7.938,
     'b_up': 6.91,
     'b_down': 50.357,
     'ln2_g': 22.319,
     'ln2_b': 22.109,
     'ssm_d': 3.602,
     'w_glu': 3.12}
    for name, (base, spread) in spreads.items():
        noise = np.random.default_rng([zlib.crc32(name.encode()), seed]).standard_normal(out[name].shape)
        drawn = base * np.exp(spread * noise) if base else spread * noise
        out[name] = __import__('jax').numpy.asarray(drawn.astype(out[name].dtype))
    for name, factor in factors.items():
        out[name] = (out[name] * factor).astype(out[name].dtype)
    return out
```

```python
import math
from collections import namedtuple
from contextlib import ExitStack

import numpy as np

import concourse.bass as bass
from concourse import mybir

F32 = mybir.dt.float32
F32R = mybir.dt.float32r
I32 = mybir.dt.int32
ALU = mybir.AluOpType
ACT = mybir.ActivationFunctionType
AX = mybir.AxisListType

P = 128
S = 512
D = 1024
M = 256
KD = D // P
ST = S // P
MT = M // P
CW = D // 2
CT = CW // P
HEADS = CT
GROUPS, GCH, NST = 32, 16, 64
PAIRS = GROUPS // 2
L = 8
NCH = S // L
BLK = CT
BP = PAIRS // BLK
BG = 2 * BP
UNIT = 1024
RING, RING2, RAW2 = 5, 8, 4
ALPHA = 2.0 ** 0.25
EPS = 1e-5
SCALE = float(P) ** -0.5
GATE_COLS = 3 * D
CONV_COL, U_COL, Q_COL = GATE_COLS, GATE_COLS + 3 * CW, GATE_COLS + 4 * CW

LR, LI, LDT, BGATE, BUP, CONVW = 0, 16, 32, 48, 72, 104
N_VEC = CONVW + 3 * CT

STEPS = [("X", 0), ("X", 1), ("k", 0), ("k", 1), ("X", 2), ("prm", 0), ("k", 2), ("X", 3), ("k", 3), ("X", 4),
         ("C", 0), ("X", 5), ("split", 0), ("ssm", 0), ("v", 0), ("ssm", 1), ("v", 1), ("ssm", 2), ("q", 0), ("ssm", 3),
         ("q", 1), ("ssm", 4), ("S", 0), ("ssm", 5), ("q", 2), ("S", 1), ("T", 0), ("q", 3), ("O", 0), ("S", 2), ("T", 1), ("u", 0), ("O", 1), ("S", 3), ("T", 2),
         ("u", 1), ("O", 2), ("T", 3), ("u", 2), ("O", 3), ("u", 3), ("c", 0),
         ("UT", 0), ("UT", 1), ("UT", 2), ("UT", 3), ("QT", 0), ("KM", 0), ("V", 0), ("c", 1), ("c", 2),
         ("Y", 0), ("QT", 1), ("KM", 1), ("V", 1), ("c", 3), ("YT", 0), ("c", 4), ("c", 5),
         ("Y", 1), ("QT", 2), ("KM", 2), ("V", 2), ("c", 6), ("YT", 1), ("c", 7), ("c", 8),
         ("Y", 2), ("QT", 3), ("KM", 3), ("V", 3), ("c", 9), ("YT", 2), ("c", 10), ("c", 11),
         ("Y", 3), ("YT", 3)]
TILES = [s for s in STEPS if s[0] in ("k", "v", "q", "u", "c")]
SPLIT_TILES = [s for s in TILES if s[0] in ("k", "v", "q")]

PRO_UNITS = []
for _s in TILES:
    if _s in (("v", 0), ("u", 0)):
        PRO_UNITS += [(_s[0], i) for i in range(4)]
    elif _s[0] not in "vu":
        PRO_UNITS.append(_s)
UNIT_OF = {s: n for n, s in enumerate(PRO_UNITS)}
N_PRO = len(PRO_UNITS)
N_TILES = {"k": CT, "v": MT, "q": HEADS, "u": 4, "c": 3 * CT}
MIX_UNITS = 5
OUT0 = N_PRO + MIX_UNITS * KD
FF0 = OUT0 + 8
QUARTERS, FQ_TILES, FQ_UNITS = 4, 8, 16
LEAD = 4


def row_of(step):
    return 4 * (step % 2) + 3 - step // 2


def units_after(step):
    kind, i = step
    if kind in "vu":
        return UNIT_OF[kind, 0] + (4 if i == N_TILES[kind] - 1 else 0)
    return UNIT_OF[step] + 1


def split_for(step):
    kind, i = step
    if kind in "vu" and i < N_TILES[kind] - 1:
        return UNIT_OF[kind, 0] + RING
    return min(units_after(step) + (1 if kind == "k" else LEAD), N_PRO + RING)


def parts_before(step):
    return len([x for x in TILES[:TILES.index(step) + 1] if x[0] in "vu" and x[1] < N_TILES[x[0]] - 1])


def conv_part(n):
    ct, part = divmod(n, 3)
    return ct, part, CONV_COL + (CW, 2 * CW, 0)[part] + ct * P

MAGIC = 1.5 * 2.0 ** 23
LOG2E = 1.0 / math.log(2.0)
LN2_HI, LN2_LO = 0.693359375, math.log(2.0) - 0.693359375
TWO_PI_1 = 6.28125
TWO_PI_2 = round((2 * math.pi - TWO_PI_1) * 2 ** 19) / 2.0 ** 19
TWO_PI_3 = 2 * math.pi - TWO_PI_1 - TWO_PI_2
ANGLE_MAX = 1.0e5
N_TURNS = 12
DT, MAG, ANG, CANG, SIN, COS, T1, T2, T3, T4, T5, KR, KI, RDEN, MAG8 = range(15)
PI_BELOW = 3.1415925

def place(nc, stack, plan, found):
    room = 0
    for item in plan:
        if isinstance(item, list):
            sizes = []
            for turn in item:
                with ExitStack() as inner:
                    sizes.append(place(nc, inner, turn, found))
            stack.enter_context(nc.sbuf_tensor(f"room{len(found)}", [P, max(sizes)], F32))
            room += max(sizes)
        else:
            name, dims, dt = item
            found[name] = stack.enter_context(nc.sbuf_tensor(name, [P, *dims], dt))
            room += int(np.prod(dims))
    return room


def f32(name, *dims):
    return name, dims, F32


def hi_lo(name, *dims):
    return [(name + "_hi", dims, F32R), (name + "_lo", dims, F32R)]


def buffers(nc, stack):
    attention = hi_lo("q", 2, S) + [f32("probs", ST, M)] + hi_lo("pT", MT, S)
    block_tables = [f32("Qr", BP, L, GCH), f32("Qi", BP, L, GCH), f32("W1r", BP, P), f32("W1i", BP, P),
                    f32("W3", BG, P), f32("SBr", BP, 2, NCH), f32("SBi", BP, 2, NCH), f32("vr", BP, NCH),
                    f32("vi", BP, NCH), f32("ta", BP, NCH), f32("tb", BP, NCH), f32("cc", S), f32("cy", S)]
    ssm = [f32("Br", PAIRS, GCH), f32("Bi", PAIRS, GCH),
           f32("CT", 2, PAIRS, GCH), f32("BDr", BP, 2, GCH), f32("BDi", BP, 2, GCH),
           f32("pwr", L + 1, PAIRS), f32("pwi", L + 1, PAIRS), f32("rvr", L, PAIRS), f32("rvi", L, PAIRS), f32("sm", 18, PAIRS), ("smi", (PAIRS,), I32),
           f32("Din", PAIRS), f32("patt", GCH), f32("DD", BP, GCH), f32("Pr", PAIRS, NCH),
           f32("Pi", PAIRS, NCH), f32("M8", BP, NCH), f32("CAr", 2, BP, L + 1, GCH),
           f32("CAi", 2, BP, L + 1, GCH), f32("Km", BP, P), f32("U8", GROUPS, NCH),
           f32("Yn", L, BP, GCH), f32("cz", S + 2 * NCH), f32("pool_tmp", 2, L + 1, GCH)]
    plan = [
        f32("ident", P), f32("prmT", N_VEC), f32("small", 64),
        *hi_lo("xT", KD, S),
        f32("raw", RING, UNIT), *hi_lo("w", RING, UNIT),
        [[*hi_lo("o", CT, S), [[*hi_lo("kT", HEADS, M), *hi_lo("v", MT, CW)], hi_lo("ys", CT, S)],
          [hi_lo("memT", KD, M), [f32("uN", GROUPS, 4, GCH)], hi_lo("z", CT, S)]],
         [*hi_lo("w2", RING2 - RING, UNIT), f32("ln1g", D), f32("ln1b", D), f32("ln2g", D), f32("ln2b", D),
          f32("bdown", D)]],
        [[[[f32("xs", MT + ST, D)], attention, block_tables], *ssm],
         [*hi_lo("m", KD, S), f32("sg", 4, S), f32("mm", 2, S), f32("x1b", D), f32("acc", ST, D)]],
    ]
    found = {}
    place(nc, stack, plan, found)
    return namedtuple("Buffers", found)(**found)


SEMAPHORES = """
    ident_ready zeros_ready bd_zero cz_zero dt_rows vec_in b_in c_in d_in
    rows_T rows_hi rows_lo vecs_T vecs_cols c_T c_cols
    w_hi_ready w_lo_ready w_used part_done pro_hi bank_out
    scores_done neg_max exps_done probs_norm probs_T pT_hi_ready pT_lo_ready o_done o_hi_ready o_lo_ready
    angles sines bbar powers phase8 turns ca_ready q_tab bd_ready
    qt_done w1_ready km_done km_ready v_done y_done sb_ready ut_done u8_ready gelu_done yt_done ys_hi_ready ys_lo_ready
    z_hi_ready z_lo_ready
    ya_done ga_done gates_out merged merge_chain m_lo_ready
    acc_in vecs_in rows_done rows_free var_ready sd_ready x1_ready x1_T x1T_hi x1T_lo acc_ready
    up_free sq_ready h_hi_ready h_lo_ready y_ready
    dve_chain pool_chain
""".split()


def build(nc, x, mem, w_in, b_gate, conv_w, w_conv_out, lam_re, lam_im, log_dt, b_re, b_im, c_re, c_im,
          ssm_d, w_glu, w_kv, w_xo, w_out, ln1_g, ln1_b, w_up, b_up, w_down, b_down, ln2_g, ln2_b, out):
    with ExitStack() as stack:
        t = buffers(nc, stack)
        banks = [stack.enter_context(nc.psum_tensor(f"bank{i}", [P, S], F32)) for i in range(8)]
        s = namedtuple("Semaphores", SEMAPHORES)(*[stack.enter_context(nc.semaphore(n)) for n in SEMAPHORES])

        def several(name, n):
            return [stack.enter_context(nc.semaphore(f"{name}{i}")) for i in range(n)]

        rows_in = several("rows_in", MT + ST)
        raw_pro, raw_mix, raw_late = several("raw_pro", RING), several("raw_mix", RING), several("raw_late", RAW2)
        w3_in = several("w3_in", BLK)
        out_in = several("out_in", ST)

        rmax, nmax, rsum, rinv = (t.small[:, 4 * i:4 * i + 4] for i in range(4))
        bn6 = t.small[:, 16:28]
        mv, ve, sd, ry, rt = t.small[:, 28:30], t.small[:, 30:31], t.small[:, 31:32], t.small[:, 32:33], t.small[:, 33:34]

        x_rows = x.rearrange("b (k t a) d -> (b t) a k d", t=ST, a=2)
        mem_rows = mem.rearrange("b (t p) d -> (b t) p d", p=P)
        out_rows = out.rearrange("b (k t a) d -> (b t) a k d", t=ST, a=2)
        ktiles = {k: w[0].rearrange("(t p) n -> p t n", p=P) for k, w in (
            ("in", w_in), ("kv", w_kv), ("conv", w_conv_out), ("xo", w_xo), ("glu", w_glu), ("out", w_out),
            ("up", w_up), ("down", w_down))}

        def pro_slot(n):
            return (n - N_PRO) % RING

        def split_slot(k):
            if k < RING:
                return t.w_hi[:, k, :], t.w_lo[:, k, :]
            return t.w2_hi[:, k - RING, :], t.w2_lo[:, k - RING, :]

        def tile_of(slot, i):
            hi, lo = split_slot(slot)
            return hi[:, i * P:(i + 1) * P], lo[:, i * P:(i + 1) * P]

        def half_of(slot, i):
            hi, lo = split_slot(slot)
            return hi[:, i * S:(i + 1) * S], lo[:, i * S:(i + 1) * S]

        prm = t.Yn[:, 0:2].rearrange("p j q c -> p (j q c)")
        ldt = t.Yn[:, 2, 0, 0:2]
        c_rows = t.Km

        def x1_slot(st):
            return t.mm[:].rearrange("p a n -> p (a n)") if st % 2 == 0 else t.x1b[:]

        def mm3(ps, lhs, rhs, first, last):
            nc.tensor.matmul(ps, lhs[0], rhs[0], start=first, stop=False)
            nc.tensor.matmul(ps, lhs[0], rhs[1], start=False, stop=False)
            return nc.tensor.matmul(ps, lhs[1], rhs[0], start=False, stop=last)

        block = stack.enter_context(nc.Block())

        @block.sync
        def _(sp):
            def load_rows(r):
                src = mem_rows[r] if r < MT else x_rows[r - MT]
                sp.dma_start(t.xs[:, r, :], src).then_inc(rows_in[r], 16)

            def load_pro(n):
                kind, i = PRO_UNITS[n]
                if n >= RING:
                    sp.wait_ge(s.w_lo_ready, n - RING + 1)
                if kind == "v":
                    src = ktiles["kv"][:, 2 * i:2 * i + 2, CW:2 * CW]
                elif kind == "u":
                    src = ktiles["in"][:, 2 * i:2 * i + 2, U_COL:U_COL + CW]
                elif kind == "k":
                    src = ktiles["kv"][:, :, i * P:(i + 1) * P]
                else:
                    col = Q_COL + i * P if kind == "q" else conv_part(i)[2]
                    src = ktiles["in"][:, :, col:col + P]
                dst = t.raw[:, pro_slot(n), :].rearrange("p (t n) -> p t n", t=src.shape[1])
                sp.dma_start(dst, src).then_inc(raw_pro[pro_slot(n)], 16)

            load_rows(0)
            load_rows(1)
            load_pro(0)
            load_pro(1)
            load_rows(2)
            load_pro(2)
            load_rows(3)
            load_pro(3)
            load_rows(4)
            load_rows(5)
            for n in range(4, N_PRO):
                load_pro(n)
            with sp.Fori(0, KD) as i:
                for k in range(MIX_UNITS):
                    sp.wait_ge(s.w_lo_ready, i * MIX_UNITS + (N_PRO + k - RING + 1))
                    if k < 3:
                        sp.dma_start(t.raw[:, k, :].rearrange("p (t n) -> p t n", t=KD),
                                     ktiles["in"][:, :, bass.ds(i * P + k * D, P)]).then_inc(raw_mix[k], 16)
                    else:
                        parts = ((ktiles["conv"], 0), (ktiles["xo"], 0)) if k == 3 else ((ktiles["glu"], 0), (ktiles["glu"], D))
                        for h, (w, col) in enumerate(parts):
                            sp.dma_start(t.raw[:, k, h * S:(h + 1) * S].rearrange("p (t n) -> p t n", t=CT),
                                         w[:, :, bass.ds(i * P + col, P)]).then_inc(raw_mix[k], 16)
            for m in range(8):
                dh, kk = divmod(m, 4)
                sp.wait_ge(s.w_lo_ready, OUT0 + m - RAW2 + 1)
                sp.dma_start(t.raw[:, m % RAW2, :].rearrange("p (t n) -> p t n", t=2),
                             ktiles["out"][:, 2 * kk:2 * kk + 2, dh * S:(dh + 1) * S]).then_inc(raw_late[m % RAW2], 16)
            with sp.Fori(0, QUARTERS) as q:
                for r in range(FQ_UNITS):
                    sp.wait_ge(s.w_lo_ready, q * FQ_UNITS + (FF0 + r - RAW2 + 1))
                    if r < FQ_TILES:
                        sp.dma_start(t.raw[:, r % RAW2, :].rearrange("p (t n) -> p t n", t=KD),
                                     ktiles["up"][:, :, bass.ds(q * (FQ_TILES * P) + r * P, P)]).then_inc(raw_late[r % RAW2], 16)
                    else:
                        dh, kk = divmod(r - FQ_TILES, 4)
                        sp.dma_start(t.raw[:, r % RAW2, :].rearrange("p (t n) -> p t n", t=2),
                                     ktiles["down"][:, bass.ds(q * FQ_TILES + 2 * kk, 2), dh * S:(dh + 1) * S]
                                     ).then_inc(raw_late[r % RAW2], 16)
            for st in range(ST):
                for h in range(2):
                    half = slice(h * S, (h + 1) * S)
                    sp.wait_ge(s.y_ready, 2 * st + h + 1)
                    sp.dma_start(out_rows[st, :, :, half], t.acc[:, st, half]).then_inc(out_in[st], 16)
            for st in range(ST):
                sp.wait_ge(out_in[st], 2 * 16)

        @block.gpsimd
        def _(pool):
            links = [0]

            def link(ins):
                ins.then_inc(s.pool_chain, 1)
                links[0] += 1
                pool.wait_ge(s.pool_chain, links[0])

            link(pool.memset(t.ident[:], 0.0))
            pool.affine_select(out=t.ident[:], in_=t.ident[:], compare_op=ALU.not_equal, fill=1.0, base=0,
                               pattern=[[-1, P]], channel_multiplier=1).then_inc(s.ident_ready, 1)

            with nc.allow_non_contiguous_dma(reason="small per-channel vectors"):
                for g in range(2):
                    half = slice(g * NST, (g + 1) * NST)
                    pool.dma_start(prm[LR:LR + PAIRS, half], lam_re[0].rearrange("(b g q) n -> g b q n", g=2, q=BP)[g]).then_inc(s.vec_in, 16)
                    pool.dma_start(prm[LI:LI + PAIRS, half], lam_im[0].rearrange("(b g q) n -> g b q n", g=2, q=BP)[g]).then_inc(s.vec_in, 16)
                    pool.dma_start(ldt[LDT:LDT + PAIRS, g:g + 1],
                                  log_dt[0].rearrange("(b g q e) -> g b q e", g=2, q=BP, e=1)[g]).then_inc(s.vec_in, 16)
                pool.dma_start(prm[BGATE:BUP, :], b_gate[0].rearrange("(c p) -> c p", p=P)).then_inc(s.vec_in, 16)
                pool.dma_start(prm[BUP:CONVW, :], b_up[0].rearrange("(c p) -> c p", p=P)).then_inc(s.vec_in, 16)
                pool.dma_start(prm[CONVW:N_VEC, :], conv_w[0].rearrange("k (c p) -> (k c) p", p=P)).then_inc(s.vec_in, 16)
                for c, w in enumerate((c_re, c_im)):
                    rows = w[0].rearrange("(t b g q) o n -> t g b (q o) n", t=2, b=2, g=2)
                    for h in range(2):
                        for g in range(2):
                            pool.dma_start(c_rows[:, 2 * c + h, g * NST:(g + 1) * NST], rows[h, g]).then_inc(s.c_in, 16)
                for dst, w in ((t.Br, b_re), (t.Bi, b_im)):
                    for g in range(2):
                        for b in range(BLK):
                            pool.dma_start(dst[g * NST:(g + 1) * NST, b * BP:(b + 1) * BP, :],
                                          w[0].rearrange("(b g q) n c -> b g n q c", g=2, q=BP)[b, g]).then_inc(s.b_in, 16)
                for g in range(2):
                    for b in range(BLK):
                        pool.dma_start(t.Din[g * GCH:(g + 1) * GCH, b * BP:(b + 1) * BP],
                                      ssm_d[0].rearrange("(b g q c) -> b g c q", g=2, q=BP, c=GCH)[b, g]).then_inc(s.d_in, 16)

            def cmul(dr, di, ar, ai, br, bi, tmp, done):
                link(pool.tensor_tensor(dr, ar, br, ALU.mult))
                link(pool.tensor_tensor(tmp, ai, bi, ALU.mult))
                link(pool.tensor_tensor(dr, dr, tmp, ALU.subtract))
                link(pool.tensor_tensor(di, ar, bi, ALU.mult))
                link(pool.tensor_tensor(tmp, ai, br, ALU.mult))
                pool.tensor_tensor(di, di, tmp, ALU.add).then_inc(done, 1)

            def c_powers(b):
                if b >= 2:
                    pool.wait_ge(s.y_done, b - 1)
                for h in range(2):
                    if b or h:
                        pool.wait_ge(s.ca_ready, 2 * b + h)
                    pairs = slice(b * BP + 2 * h, b * BP + 2 * h + 2)
                    dims = [P, 2, L + 1, GCH]
                    ar = t.pwr[:].rearrange("p l q -> p q l")[:, pairs, :].unsqueeze(3).broadcast_to(dims)
                    ai = t.pwi[:].rearrange("p l q -> p q l")[:, pairs, :].unsqueeze(3).broadcast_to(dims)
                    cr = t.CT[:, 0, pairs, :].unsqueeze(2).broadcast_to(dims)
                    ci = t.CT[:, 1, pairs, :].unsqueeze(2).broadcast_to(dims)
                    cmul(t.CAr[:, b % 2, 2 * h:2 * h + 2], t.CAi[:, b % 2, 2 * h:2 * h + 2], ar, ai, cr, ci,
                         t.pool_tmp[:], s.ca_ready)

            def input_powers(b):
                if b:
                    pool.wait_ge(s.qt_done, 2 * b)
                for h in range(2):
                    pairs = slice(b * BP + 2 * h, b * BP + 2 * h + 2)
                    dims = [P, 2, L, GCH]
                    ar = t.rvr[:].rearrange("p l q -> p q l")[:, pairs, :].unsqueeze(3).broadcast_to(dims)
                    ai = t.rvi[:].rearrange("p l q -> p q l")[:, pairs, :].unsqueeze(3).broadcast_to(dims)
                    br = t.Br[:, pairs, :].unsqueeze(2).broadcast_to(dims)
                    bi = t.Bi[:, pairs, :].unsqueeze(2).broadcast_to(dims)
                    pool.wait_ge(s.ca_ready, 2 * b + 2)
                    if b or h:
                        pool.wait_ge(s.q_tab, 2 * b + h)
                    cmul(t.Qr[:, 2 * h:2 * h + 2], t.Qi[:, 2 * h:2 * h + 2], ar, ai, br, bi,
                         t.pool_tmp[:, :, 0:L, :], s.q_tab)

            link(pool.memset(t.BDr[:], 0.0))
            link(pool.memset(t.BDi[:], 0.0))
            link(pool.memset(t.M8[:], 0.0))
            link(pool.memset(t.Pr[:, :, 0], 1.0))
            pool.memset(t.Pi[:, :, 0], 0.0).then_inc(s.bd_zero, 1)
            pool.wait_ge(s.c_cols, 1)
            pool.wait_ge(s.powers, 4)
            c_powers(0)
            pool.wait_ge(s.phase8, 1)
            pool.wait_ge(s.ca_ready, 2)
            m, n_turns = 1, 0
            while m < NCH - 1:
                n = min(m, NCH - 1 - m)
                for h in range(2):
                    half = slice(h * PAIRS // 2, (h + 1) * PAIRS // 2)
                    dims = [P, PAIRS // 2, n]
                    cmul(t.Pr[:, half, m + 1:m + 1 + n], t.Pi[:, half, m + 1:m + 1 + n],
                         t.Pr[:, half, 1:1 + n], t.Pi[:, half, 1:1 + n],
                         t.Pr[:, half, m:m + 1].broadcast_to(dims), t.Pi[:, half, m:m + 1].broadcast_to(dims),
                         t.pool_tmp[:].rearrange("p a l c -> p (a l c)")[:, 0:n * PAIRS // 2].rearrange("p (q n) -> p q n", n=n),
                         s.turns)
                    n_turns += 1
                    pool.wait_ge(s.turns, n_turns)
                m += n
            assert n_turns == N_TURNS
            pool.wait_ge(s.o_done, HEADS)
            link(pool.memset(t.W3[:], 0.0))
            link(pool.memset(t.SBr[:], 0.0))
            pool.memset(t.SBi[:], 0.0).then_inc(s.zeros_ready, 1)
            pool.wait_ge(s.bbar, 1)
            for b in range(BLK):
                input_powers(b)
                if b + 1 < BLK:
                    pool.wait_ge(s.q_tab, 2 * b + 2)
                    c_powers(b + 1)
            pool.wait_ge(s.ys_lo_ready, BLK)
            for st in range(ST):
                pool.dma_start(t.acc[:, st, :], x_rows[st]).then_inc(s.acc_in, 16)
            pool.wait_ge(s.w_used, OUT0)
            for dst, src in ((t.ln1g, ln1_g), (t.ln1b, ln1_b), (t.bdown, b_down), (t.ln2g, ln2_g), (t.ln2b, ln2_b)):
                pool.dma_start(dst[:], src[0].partition_broadcast(P)).then_inc(s.vecs_in, 16)
            pool.wait_ge(s.vecs_in, 5 * 16)
            for st in range(ST):
                pool.wait_ge(s.x1_ready, 2 * st + 2)
                link(pool.tensor_scalar(t.acc[:, st, :], x1_slot(st), ALPHA, None, ALU.mult))
                pool.tensor_tensor(t.acc[:, st, :], t.acc[:, st, :], t.bdown[:], ALU.add).then_inc(s.acc_ready, 1)

        @block.tensor
        def _(pe):
            def weights(n):
                pe.wait_ge(s.w_lo_ready, n + 1)

            def turn(out, rows, h):
                return pe.matmul(out, rows, t.ident[h, h], start=True, stop=True)

            pe.wait_ge(s.ident_ready, 1)
            for kind, i in STEPS:
                if kind in ("k", "v", "q", "u", "c"):
                    idx = TILES.index((kind, i))
                    ps = banks[(idx + 2) % 3]
                    if idx >= 3:
                        pe.wait_ge(s.bank_out, idx - 2)
                if kind == "X":
                    pe.wait_ge(rows_in[i], 16)
                    for h in range(2):
                        g = 2 * i + h
                        if g >= 3:
                            pe.wait_ge(s.rows_lo, g - 2)
                        for k in range(4):
                            kt = 4 * h + k
                            last = pe.transpose(banks[3 + g % 3][:, k * P:(k + 1) * P], t.xs[:, i, kt * P:(kt + 1) * P], t.ident[:])
                        last.then_inc(s.rows_T, 1)
                elif kind == "prm":
                    pe.wait_ge(s.dt_rows, 1)
                    pe.transpose(banks[7][:, 0:N_VEC], prm[0:N_VEC, :], t.ident[0:N_VEC, 0:N_VEC]).then_inc(s.vecs_T, 1)
                elif kind == "C":
                    pe.wait_ge(s.c_in, 8 * 16)
                    for k in range(4):
                        last = pe.transpose(banks[6][:, k * P:(k + 1) * P], c_rows[:, k, :], t.ident[:])
                    last.then_inc(s.c_T, 1)
                elif kind == "k":
                    weights(UNIT_OF[kind, i])
                    pe.wait_ge(s.rows_lo, 2 * MT)
                    for kt in range(KD):
                        last = mm3(ps[:, 0:M], tile_of(pro_slot(UNIT_OF[kind, i]), kt),
                                   (t.memT_hi[:, kt, :], t.memT_lo[:, kt, :]), kt == 0, kt == KD - 1)
                    last.then_inc(s.w_used, 1)
                elif kind in ("v", "u"):
                    if kind == "u":
                        pe.wait_ge(s.rows_lo, 2 * (MT + ST))
                    for kt in range(KD):
                        n = UNIT_OF[kind, 0] + kt // 2
                        weights(n)
                        if kind == "v":
                            rows = [a[:, kt, i * P:(i + 1) * P] for a in (t.memT_hi, t.memT_lo)]
                        else:
                            rows = [a[:, kt, i * P:(i + 1) * P] for a in (t.xT_hi, t.xT_lo)]
                        last = mm3(ps[:, :], rows, half_of(pro_slot(n), kt % 2), kt == 0, kt == KD - 1)
                        if i == N_TILES[kind] - 1 and kt % 2:
                            last.then_inc(s.w_used, 1)
                    if i < N_TILES[kind] - 1:
                        last.then_inc(s.part_done, 1)
                elif kind in ("q", "c"):
                    weights(UNIT_OF[kind, i])
                    pe.wait_ge(s.rows_lo, 2 * (MT + ST))
                    for kt in range(KD):
                        last = mm3(ps[:, :], tile_of(pro_slot(UNIT_OF[kind, i]), kt),
                                   (t.xT_hi[:, kt, :], t.xT_lo[:, kt, :]), kt == 0, kt == KD - 1)
                    last.then_inc(s.w_used, 1)
                elif kind == "S":
                    pe.wait_ge(s.bank_out, TILES.index(("q", i)) + 1)
                    if i:
                        pe.wait_ge(s.exps_done, 4 * i)
                    for st in range(ST):
                        q = [a[:, i % 2, st * P:(st + 1) * P] for a in (t.q_hi, t.q_lo)]
                        last = mm3(banks[3 + st // 2][:, (st % 2) * M:(st % 2 + 1) * M], q,
                                   (t.kT_hi[:, i, :], t.kT_lo[:, i, :]), True, True)
                        if st % 2:
                            last.then_inc(s.scores_done, 1)
                elif kind == "T":
                    pe.wait_ge(s.probs_norm, i + 1)
                    if i:
                        pe.wait_ge(s.pT_lo_ready, 2 * i)
                    for mt in range(MT):
                        for st in range(ST):
                            last = pe.transpose(banks[5 + mt][:, st * P:(st + 1) * P], t.probs[:, st, mt * P:(mt + 1) * P], t.ident[:])
                        last.then_inc(s.probs_T, 1)
                elif kind == "O":
                    pe.wait_ge(s.pT_lo_ready, 2 * i + 2)
                    if i:
                        pe.wait_ge(s.o_lo_ready, i)
                    for mt in range(MT):
                        v = [a[:, mt, i * P:(i + 1) * P] for a in (t.v_hi, t.v_lo)]
                        last = mm3(banks[7][:, :], v, (t.pT_hi[:, mt, :], t.pT_lo[:, mt, :]), mt == 0, mt == MT - 1)
                    last.then_inc(s.o_done, 1)
                elif kind == "UT":
                    pe.wait_ge(s.bank_out, TILES.index(("u", 3)) + 1)
                    if i >= 2:
                        pe.wait_ge(s.u8_ready, i - 1)
                    for g in range(BG):
                        for a in range(2):
                            h = slice(a * NCH, (a + 1) * NCH)
                            last = turn(banks[3 + i % 2][h, g * NCH:(g + 1) * NCH], t.uN[h, i * BG + g].rearrange("p l c -> p (l c)"), h)
                    last.then_inc(s.ut_done, 1)
                elif kind == "YT":
                    pe.wait_ge(s.gelu_done, i + 1)
                    pe.wait_ge(s.km_ready, min(i + 2, BLK))
                    for j in range(L):
                        for g in range(2):
                            h = slice(g * NCH, (g + 1) * NCH)
                            last = turn(banks[5][h, j * NCH:(j + 1) * NCH], t.Yn[h, j].rearrange("p q c -> p (q c)"), h)
                    last.then_inc(s.yt_done, 1)
                elif kind == "QT":
                    pe.wait_ge(s.q_tab, 2 * i + 2)
                    if i == 0:
                        pe.wait_ge(s.u8_ready, BLK)
                    if i:
                        pe.wait_ge(s.w1_ready, 2 * i)
                    for c, tab in enumerate((t.Qr, t.Qi)):
                        for q in range(BP):
                            last = pe.transpose(banks[3 + c][:, q * P:(q + 1) * P],
                                                tab[:, q].rearrange("p l c -> p (l c)"), t.ident[:])
                        last.then_inc(s.qt_done, 1)
                elif kind == "KM":
                    pe.wait_ge(s.bd_ready, i + 1)
                    pe.wait_ge(s.ca_ready, 2 * i + 2)
                    if i:
                        pe.wait_ge(s.km_ready, i)
                    if i >= 2:
                        pe.wait_ge(s.ys_lo_ready, i - 1)
                    for q in range(BP):
                        ca = [a[:, i % 2, q, 0:L, :].rearrange("p l c -> p (l c)") for a in (t.CAr, t.CAi)]
                        pe.matmul(banks[5][0:2 * GCH, q * P:(q + 1) * P], t.BDr[:, q].rearrange("p g c -> p (g c)"), ca[0],
                                  start=True, stop=False)
                        last = pe.matmul(banks[5][0:2 * GCH, q * P:(q + 1) * P], t.BDi[:, q].rearrange("p g c -> p (g c)"), ca[1],
                                         start=False, stop=True)
                    last.then_inc(s.km_done, 1)
                elif kind == "V":
                    pe.wait_ge(s.w1_ready, 2 * i + 2)
                    pe.wait_ge(s.u8_ready, i + 1)
                    if i:
                        pe.wait_ge(s.sb_ready, i)
                    for q in range(BP):
                        for g in range(2):
                            half = slice(g * NST, (g + 1) * NST)
                            for c, w in enumerate((t.W1r, t.W1i)):
                                last = pe.matmul(banks[6][half, c * BP * NCH + q * NCH:c * BP * NCH + (q + 1) * NCH],
                                                 w[:, q, half], t.U8[:, i * BG + g * BP + q, :], start=True, stop=True)
                    last.then_inc(s.v_done, 1)
                elif kind == "Y":
                    pe.wait_ge(s.sb_ready, i + 1)
                    pe.wait_ge(w3_in[i], 2 * L * 16)
                    if i:
                        pe.wait_ge(s.gelu_done, i)
                    for q in range(BP):
                        ps = banks[7][:, q * P:(q + 1) * P]
                        ca = [a[:, i % 2, q, 1:L + 1, :].rearrange("p l c -> p (l c)") for a in (t.CAr, t.CAi)]
                        pe.matmul(ps, t.SBr[:, q].rearrange("p g k -> p (g k)"), ca[0], start=True, stop=False)
                        pe.matmul(ps, t.SBi[:, q].rearrange("p g k -> p (g k)"), ca[1], start=False, stop=False)
                        for g in range(2):
                            last = pe.matmul(banks[7][g * NCH:(g + 1) * NCH, q * P:(q + 1) * P], t.U8[:, i * BG + g * BP + q, :],
                                             t.W3[:, g * BP + q, :], start=False, stop=True)
                    last.then_inc(s.y_done, 1)

            pe.wait_ge(s.bank_out, len(TILES))
            with pe.Fori(0, KD) as i:
                for k in range(MIX_UNITS):
                    pe.wait_ge(s.w_lo_ready, i * MIX_UNITS + (N_PRO + k + 1))
                    if k < 3:
                        for kt in range(KD):
                            last = mm3(banks[k][:, :], tile_of(k, kt), (t.xT_hi[:, kt, :], t.xT_lo[:, kt, :]), kt == 0, kt == KD - 1)
                        last.then_inc(s.w_used, 1)
                        continue
                    for h in range(2):
                        bank = 3 + 2 * (k - 3) + h
                        if bank < 6:
                            pe.wait_ge(s.bank_out, i * 3 + (len(TILES) + bank - 5))
                        if k == 3 and h == 0:
                            pe.wait_ge(s.z_lo_ready, CT)
                            src = (t.z_hi, t.z_lo)
                        elif k == 3:
                            pe.wait_ge(s.o_lo_ready, HEADS)
                            src = (t.o_hi, t.o_lo)
                        else:
                            pe.wait_ge(s.ys_lo_ready, BLK)
                            src = (t.ys_hi, t.ys_lo)
                        for kt in range(CT):
                            last = mm3(banks[bank][:, :], tile_of(k, h * CT + kt), (src[0][:, kt, :], src[1][:, kt, :]), kt == 0, kt == CT - 1)
                        last.then_inc(s.w_used if h else (s.ya_done, s.ga_done)[k - 3], 1)

            def transpose_x1(st):
                for h in range(2):
                    pe.wait_ge(s.x1_ready, 2 * st + h + 1)
                    for k in range(4):
                        kt = 4 * h + k
                        last = pe.transpose(banks[2 * st + h][:, k * P:(k + 1) * P], x1_slot(st)[:, kt * P:(kt + 1) * P], t.ident[:])
                    last.then_inc(s.x1_T, 1)

            for step in range(8):
                st, dh = divmod(step, 2)
                if step in (0, 1, 2, 6):
                    pe.wait_ge(s.gates_out, 4 * (KD - 1) + min(step, 3) + 1)
                elif step < 6:
                    pe.wait_ge(s.bank_out, len(TILES) + 3 * (KD - 1) + step - 2)
                for kt in range(KD):
                    u = 4 * dh + kt // 2
                    if st == 0:
                        pe.wait_ge(s.w_lo_ready, OUT0 + u + 1)
                    if step == 0:
                        pe.wait_ge(s.m_lo_ready, kt + 1)
                    last = mm3(banks[step][:, :], (t.m_hi[:, kt, st * P:(st + 1) * P], t.m_lo[:, kt, st * P:(st + 1) * P]),
                               half_of(u, kt % 2), kt == 0, kt == KD - 1)
                    if st == ST - 1 and kt % 2:
                        last.then_inc(s.w_used, 1)
                if st < ST - 1:
                    last.then_inc(s.rows_done, 1)
                if step in (3, 5, 7):
                    transpose_x1(st - 1)
            transpose_x1(ST - 1)

            pe.wait_ge(s.x1T_lo, 2 * ST)
            with pe.Fori(0, QUARTERS) as q:
                for r in range(FQ_TILES):
                    pe.wait_ge(s.w_lo_ready, q * FQ_UNITS + (FF0 + r + 1))
                    pe.wait_ge(s.rows_free, q * 8 + (r + 1))
                    for kt in range(KD):
                        last = mm3(banks[r][:, :], tile_of(r, kt), (t.xT_hi[:, kt, :], t.xT_lo[:, kt, :]), kt == 0, kt == KD - 1)
                    last.then_inc(s.w_used, 1)
                for step in range(8):
                    st, dh = divmod(step, 2)
                    pe.wait_ge(s.up_free, q * FQ_TILES + (step + 1))
                    for kt in range(KD):
                        u = 4 * dh + kt // 2
                        if st == 0:
                            pe.wait_ge(s.w_lo_ready, q * FQ_UNITS + (FF0 + FQ_TILES + u + 1))
                        if step == 0:
                            pe.wait_ge(s.h_lo_ready, q * FQ_TILES + (kt + 1))
                        last = mm3(banks[step][:, :], (t.m_hi[:, kt, st * P:(st + 1) * P], t.m_lo[:, kt, st * P:(st + 1) * P]),
                                   half_of(u, kt % 2), kt == 0, kt == KD - 1)
                        if st == ST - 1 and kt % 2:
                            last.then_inc(s.w_used, 1)
                    if st < ST - 1:
                        last.then_inc(s.rows_done, 1)

        @block.scalar
        def _(act):
            split_to = [0]

            def hi_pro(upto):
                while split_to[0] < upto:
                    n = split_to[0]
                    slot = pro_slot(n)
                    act.wait_ge((raw_pro if n < N_PRO else raw_mix)[slot],
                                16 * (n // RING + 1) if n < N_PRO else (16 if slot < 3 else 32))
                    if n >= RING:
                        act.wait_ge(s.w_used, n - RING + 1)
                    act.activation(split_slot(slot)[0], t.raw[:, slot, :], ACT.Copy).then_inc(s.w_hi_ready, 1)
                    split_to[0] += 1

            for kind, i in STEPS:
                if (kind, i) in TILES:
                    hi_pro(split_for((kind, i)))
                if kind == "split":
                    hi_pro(split_for(("v", 0)))
                if kind == "X":
                    for h in range(2):
                        g = 2 * i + h
                        act.wait_ge(s.rows_T, g + 1)
                        dst = (t.memT_hi[:, 4 * h:4 * h + 4, i * P:(i + 1) * P] if i < MT else
                               t.xT_hi[:, 4 * h:4 * h + 4, (i - MT) * P:(i - MT + 1) * P])
                        act.activation(dst, banks[3 + g % 3][:, :].rearrange("p (k n) -> p k n", n=P), ACT.Copy).then_inc(s.rows_hi, 1)
                elif (kind, i) == ("ssm", 2):
                    act.wait_ge(s.angles, 1)
                    act.activation(t.sm[:, SIN, :], t.sm[:, ANG, :], ACT.Sin).then_inc(s.sines, 1)
                    act.activation(t.sm[:, COS, :], t.sm[:, CANG, :], ACT.Sin).then_inc(s.sines, 1)
                elif kind in ("k", "v", "q"):
                    idx = TILES.index((kind, i))
                    ps = banks[(idx + 2) % 3]
                    if (kind, i) == ("v", 0):
                        act.wait_ge(s.part_done, 1)
                    else:
                        act.wait_ge(s.w_used, units_after((kind, i)))
                    if kind == "k":
                        act.activation(t.kT_hi[:, i, :], ps[:, 0:M], ACT.Copy).then_inc(s.pro_hi, 1)
                    elif kind == "v":
                        act.activation(t.v_hi[:, i, :], ps[:, :], ACT.Copy).then_inc(s.pro_hi, 1)
                    else:
                        if i == 0:
                            act.wait_ge(s.rows_T, 2 * (MT + ST))
                        if i >= 2:
                            act.wait_ge(s.scores_done, 2 * (i - 1))
                        act.activation(t.q_hi[:, i % 2, :], ps[:, :], ACT.Copy).then_inc(s.pro_hi, 1)
                elif kind == "S":
                    if i:
                        act.wait_ge(s.probs_T, 2 * i)
                    for st in range(ST):
                        act.wait_ge(s.neg_max, 2 * i + st // 2 + 1)
                        act.activation(t.probs[:, st, :], banks[3 + st // 2][:, (st % 2) * M:(st % 2 + 1) * M], ACT.Exp,
                                       bias=nmax[:, st:st + 1], scale=SCALE, accum_out=rsum[:, st:st + 1]).then_inc(s.exps_done, 1)
                elif kind == "T":
                    for mt in range(MT):
                        act.wait_ge(s.probs_T, 2 * i + mt + 1)
                        if i and mt == 0:
                            act.wait_ge(s.o_done, i)
                        act.activation(t.pT_hi[:, mt, :], banks[5 + mt][:, :], ACT.Copy).then_inc(s.pT_hi_ready, 1)
                elif kind == "O":
                    act.wait_ge(s.o_done, i + 1)
                    act.activation(t.o_hi[:, i, :], banks[7][:, :], ACT.Copy).then_inc(s.o_hi_ready, 1)
                elif kind == "UT":
                    act.wait_ge(s.ut_done, i + 1)
                    act.activation(t.U8[:, i * BG:(i + 1) * BG, :].rearrange("p g k -> p (g k)"), banks[3 + i % 2][:, :],
                                   ACT.Copy).then_inc(s.u8_ready, 1)
                elif kind == "QT":
                    for c, dst in enumerate((t.W1r, t.W1i)):
                        act.wait_ge(s.qt_done, 2 * i + c + 1)
                        act.activation(dst[:].rearrange("p q n -> p (q n)"), banks[3 + c][:, :], ACT.Copy).then_inc(s.w1_ready, 1)
                elif kind == "KM":
                    act.wait_ge(s.km_ready, i + 1)
                    act.wait_ge(s.zeros_ready, 1)
                    if i:
                        act.wait_ge(s.y_done, i)
                    for step in range(L):
                        for g in range(2):
                            act.dma_start(t.W3[row_of(step) * GCH:(row_of(step) + 1) * GCH, g * BP:(g + 1) * BP, step * GCH:P],
                                          t.Km[g * GCH:(g + 1) * GCH, :, 0:(L - step) * GCH]).then_inc(w3_in[i], 16)
                elif kind == "Y":
                    act.wait_ge(s.y_done, i + 1)
                    if i:
                        act.wait_ge(s.yt_done, i)
                    act.activation(t.Yn[:].rearrange("p j q c -> p q j c"), banks[7][:, :].rearrange("p (q j c) -> p q j c", q=BP, c=GCH),
                                   ACT.Gelu_apprx_tanh).then_inc(s.gelu_done, 1)
                elif kind == "YT":
                    act.wait_ge(s.yt_done, i + 1)
                    act.activation(t.ys_hi[:, i, :], banks[5][:, :], ACT.Copy).then_inc(s.ys_hi_ready, 1)
                elif kind == "c" and i % 3 == 2:
                    act.wait_ge(s.bank_out, TILES.index((kind, i)) + 1)
                    act.activation(t.z_hi[:, i // 3, :], t.cc[:], ACT.Copy).then_inc(s.z_hi_ready, 1)
            hi_pro(N_PRO + RING)

            act.wait_ge(s.ys_lo_ready, BLK)

            def merge_round(i, split_next):
                for k in range(MIX_UNITS):
                    if k < 3 or k == 4:
                        sg = min(k, 3)
                        bank = (0, 1, 2, None, 6)[k]
                        act.wait_ge(s.w_used, i * MIX_UNITS + (N_PRO + k + 1))
                        if k < 3:
                            act.activation(t.sg[:, sg, :], banks[bank][:, :], ACT.Sigmoid,
                                           bias=t.prmT[:, bass.ds(i + (BGATE + k * KD), 1)]).then_inc(s.gates_out, 1)
                        else:
                            act.activation(t.sg[:, sg, :], banks[bank][:, :], ACT.Sigmoid).then_inc(s.gates_out, 1)
                    split_next(k)
                act.wait_ge(s.merged, i + 1)

            with act.Fori(0, KD - 1) as i:
                def hi_mix(k):
                    act.wait_ge(raw_mix[k], i * (16 if k < 3 else 32) + (32 if k < 3 else 64))
                    act.wait_ge(s.w_used, i * MIX_UNITS + (N_PRO + k + 1))
                    act.activation(split_slot(k)[0], t.raw[:, k, :], ACT.Copy).then_inc(s.w_hi_ready, 1)
                merge_round(i, hi_mix)

            def hi_late(m, slot, count, used):
                act.wait_ge(raw_late[m % RAW2], count)
                act.wait_ge(s.w_used, used)
                act.activation(split_slot(slot)[0], t.raw[:, m % RAW2, :], ACT.Copy).then_inc(s.w_hi_ready, 1)

            merge_round(KD - 1, lambda k: hi_late(k, k, 16 * (k // RAW2 + 1), OUT0 - MIX_UNITS + k + 1))
            for k in range(RING, RING2):
                hi_late(k, k, 16 * (k // RAW2 + 1), OUT0)

            def sqrt_var(n):
                act.wait_ge(s.var_ready, n + 1)
                act.activation(sd, ve, ACT.Sqrt).then_inc(s.sd_ready, 1)

            def hi_x1(st):
                for h in range(2):
                    act.wait_ge(s.x1_T, 2 * st + h + 1)
                    act.activation(t.xT_hi[:, 4 * h:4 * h + 4, st * P:(st + 1) * P],
                                   banks[2 * st + h][:, :].rearrange("p (k n) -> p k n", n=P), ACT.Copy).then_inc(s.x1T_hi, 1)

            for st in range(ST):
                sqrt_var(st)
                if st:
                    hi_x1(st - 1)
            for k in range(4):
                hi_late(8 + k, k, 16 * ((8 + k) // RAW2 + 1), OUT0 + k + 1)
            hi_x1(ST - 1)
            for k in range(4, 8):
                hi_late(8 + k, k, 16 * ((8 + k) // RAW2 + 1), OUT0 + k + 1)

            def quarter(q, last):
                for r in range(FQ_TILES):
                    act.wait_ge(s.w_used, q * FQ_UNITS + (FF0 + r + 1))
                    if r >= 2:
                        act.wait_ge(s.h_lo_ready, q * FQ_TILES + (r - 1))
                    act.activation(t.sg[:, r % 2, :], banks[r][:, :], ACT.Relu,
                                   bias=t.prmT[:, bass.ds(q * FQ_TILES + (BUP + r), 1)]).then_inc(s.up_free, 1)
                    act.wait_ge(s.up_free, q * FQ_TILES + (r + 1))
                    act.activation(t.sg[:, 2 + r % 2, :], t.sg[:, r % 2, :], ACT.Square).then_inc(s.sq_ready, 1)
                    hi_late(r, r, q * (16 * FQ_UNITS // RAW2) + 16 * ((16 + r) // RAW2 + 1), q * FQ_UNITS + (FF0 + r + 1))
                if not last:
                    act.wait_ge(s.h_lo_ready, q * FQ_TILES + FQ_TILES)
                    for k in range(8):
                        hi_late(k, k, q * (16 * FQ_UNITS // RAW2) + 16 * ((24 + k) // RAW2 + 1),
                                q * FQ_UNITS + (FF0 + FQ_TILES + k + 1))

            with act.Fori(0, QUARTERS - 1) as q:
                quarter(q, False)
            quarter(QUARTERS - 1, True)
            for st in range(ST):
                sqrt_var(ST + st)

        @block.vector
        def _(dve):
            links = [0]
            split_to = [0]

            def link(ins):
                ins.then_inc(s.dve_chain, 1)
                links[0] += 1
                dve.wait_ge(s.dve_chain, links[0])

            def as_f32(ap):
                return ap.bitcast(F32)

            def lo_pro(upto):
                while split_to[0] < upto:
                    n = split_to[0]
                    slot = pro_slot(n)
                    dve.wait_ge(s.w_hi_ready, n + 1)
                    hi, lo = split_slot(slot)
                    dve.tensor_tensor(lo, t.raw[:, slot, :], as_f32(hi), ALU.subtract).then_inc(s.w_lo_ready, 1)
                    split_to[0] += 1

            def sm(i):
                return t.sm[:, i, :]

            def vexp(dst, src):
                c, n, r, bits = sm(T1), sm(T2), sm(T3), t.smi[:]
                link(dve.tensor_scalar(c, src, -104.0, 89.0, ALU.max, ALU.min))
                link(dve.tensor_scalar(n, c, LOG2E, MAGIC, ALU.mult, ALU.add))
                link(dve.tensor_scalar(n, n, MAGIC, None, ALU.subtract))
                link(dve.scalar_tensor_tensor(r, n, -LN2_HI, c, ALU.mult, ALU.add))
                link(dve.scalar_tensor_tensor(r, n, -LN2_LO, r, ALU.mult, ALU.add))
                link(dve.tensor_scalar(n, n, -127.0, 128.0, ALU.max, ALU.min))
                link(dve.tensor_scalar(bits, n, 127.0, None, ALU.add))
                link(dve.tensor_scalar(bits, bits, 23, None, ALU.logical_shift_left))
                link(dve.tensor_scalar(c, r, 1.0 / math.factorial(7), None, ALU.mult))
                for k in (6, 5, 4, 3, 2, 1):
                    link(dve.scalar_tensor_tensor(c, c, 1.0 / math.factorial(k), r, ALU.add, ALU.mult))
                link(dve.scalar_tensor_tensor(dst, c, 1.0, bits.bitcast(F32), ALU.add, ALU.mult))

            def cmul(dr, di, ar, ai, br, bi, tmp):
                link(dve.tensor_tensor(dr, ar, br, ALU.mult))
                link(dve.tensor_tensor(tmp, ai, bi, ALU.mult))
                link(dve.tensor_tensor(dr, dr, tmp, ALU.subtract))
                link(dve.tensor_tensor(di, ar, bi, ALU.mult))
                link(dve.tensor_tensor(tmp, ai, br, ALU.mult))
                link(dve.tensor_tensor(di, di, tmp, ALU.add))

            lr, li, ld = (t.prmT[:, c:c + PAIRS] for c in (LR, LI, LDT))
            tmp = t.U8[:, 0:16, :].rearrange("p g k -> p (g k)").rearrange("p (n q c) -> p n q c", n=4, c=GCH)

            def step_size():
                dve.wait_ge(s.vecs_cols, 1)
                vexp(sm(DT), ld)

            def decay():
                link(dve.tensor_tensor(sm(T4), lr, sm(DT), ALU.mult))
                vexp(sm(MAG), sm(T4))

            def angle():
                link(dve.tensor_tensor(sm(ANG), li, sm(DT), ALU.mult))
                link(dve.tensor_scalar(sm(ANG), sm(ANG), -ANGLE_MAX, ANGLE_MAX, ALU.max, ALU.min))
                link(dve.tensor_scalar(sm(T1), sm(ANG), 1.0 / (2 * math.pi), MAGIC, ALU.mult, ALU.add))
                link(dve.tensor_scalar(sm(T1), sm(T1), MAGIC, None, ALU.subtract))
                for part in (TWO_PI_1, TWO_PI_2, TWO_PI_3):
                    link(dve.scalar_tensor_tensor(sm(ANG), sm(T1), -part, sm(ANG), ALU.mult, ALU.add))
                link(dve.tensor_scalar(sm(ANG), sm(ANG), -PI_BELOW, PI_BELOW, ALU.max, ALU.min))
                link(dve.scalar_tensor_tensor(sm(CANG), sm(ANG), -1.0, sm(ANG), ALU.mult, ALU.max))
                dve.tensor_scalar(sm(CANG), sm(CANG), -1.0, math.pi / 2, ALU.mult, ALU.add).then_inc(s.angles, 1)
                link(dve.tensor_tensor(sm(T1), lr, lr, ALU.mult))
                link(dve.tensor_tensor(sm(T2), li, li, ALU.mult))
                link(dve.tensor_tensor(sm(T1), sm(T1), sm(T2), ALU.add))
                link(dve.reciprocal(sm(RDEN), sm(T1)))

            def discretise():
                dve.wait_ge(s.sines, 2)
                link(dve.memset(t.pwr[:, 0, :], 1.0))
                link(dve.memset(t.pwi[:, 0, :], 0.0))
                link(dve.tensor_tensor(t.pwr[:, 1, :], sm(MAG), sm(COS), ALU.mult))
                link(dve.tensor_tensor(t.pwi[:, 1, :], sm(MAG), sm(SIN), ALU.mult))
                ai = t.pwi[:, 1, :]
                link(dve.tensor_scalar(sm(T1), t.pwr[:, 1, :], -1.0, None, ALU.add))
                link(dve.tensor_tensor(sm(KR), sm(T1), lr, ALU.mult))
                link(dve.tensor_tensor(sm(T2), ai, li, ALU.mult))
                link(dve.tensor_tensor(sm(KR), sm(KR), sm(T2), ALU.add))
                link(dve.tensor_tensor(sm(KR), sm(KR), sm(RDEN), ALU.mult))
                link(dve.tensor_tensor(sm(KI), ai, lr, ALU.mult))
                link(dve.tensor_tensor(sm(T2), sm(T1), li, ALU.mult))
                link(dve.tensor_tensor(sm(KI), sm(KI), sm(T2), ALU.subtract))
                link(dve.tensor_tensor(sm(KI), sm(KI), sm(RDEN), ALU.mult))
                dve.wait_ge(s.b_in, 2 * 2 * BLK * 16)
                dims = [P, PAIRS, GCH]
                kr, ki = (sm(k).unsqueeze(2).broadcast_to(dims) for k in (KR, KI))
                link(dve.tensor_tensor(tmp[:, 0], kr, t.Br[:], ALU.mult))
                link(dve.tensor_tensor(tmp[:, 1], ki, t.Bi[:], ALU.mult))
                link(dve.tensor_tensor(tmp[:, 2], kr, t.Bi[:], ALU.mult))
                link(dve.tensor_tensor(tmp[:, 3], ki, t.Br[:], ALU.mult))
                link(dve.tensor_tensor(t.Br[:], tmp[:, 0], tmp[:, 1], ALU.subtract))
                dve.tensor_tensor(t.Bi[:], tmp[:, 2], tmp[:, 3], ALU.add).then_inc(s.bbar, 1)
                dve.wait_ge(s.bbar, 1)

            def powers():
                m = 1
                while m < L:
                    dims = [P, m, PAIRS]
                    cmul(t.pwr[:, m + 1:2 * m + 1, :], t.pwi[:, m + 1:2 * m + 1, :], t.pwr[:, 1:m + 1, :], t.pwi[:, 1:m + 1, :],
                         t.pwr[:, m:m + 1, :].broadcast_to(dims), t.pwi[:, m:m + 1, :].broadcast_to(dims), tmp[:, 0, 0:m, :])
                    m *= 2
                for dst, src in ((t.rvr, t.pwr), (t.rvi, t.pwi)):
                    dve.tensor_copy(dst[:, 0:4, :], src[:, 1:8:2, :]).then_inc(s.powers, 1)
                    dve.tensor_copy(dst[:, 4:8, :], src[:, 0:7:2, :]).then_inc(s.powers, 1)

            def chunk_step():
                dve.wait_ge(s.bd_zero, 1)
                pr, pi = sm(COS), sm(SIN)
                for k in range(3):
                    last = k == 2
                    dr, di = (t.Pr[:, :, 1], t.Pi[:, :, 1]) if last else (sm(T3 if k else T5), sm(T4 if k else KR))
                    cmul(dr, di, pr, pi, pr, pi, sm(T1))
                    pr, pi = dr, di
                link(dve.tensor_tensor(sm(MAG8), sm(MAG), sm(MAG), ALU.mult))
                link(dve.tensor_tensor(sm(MAG8), sm(MAG8), sm(MAG8), ALU.mult))
                dve.tensor_tensor(sm(MAG8), sm(MAG8), sm(MAG8), ALU.mult).then_inc(s.phase8, 1)
                dve.wait_ge(s.phase8, 1)
                dve.wait_ge(s.d_in, 2 * BLK * 16)
                rows = slice(0, 2 * GCH)
                dve.tensor_tensor(t.patt[rows, :], t.ident[rows, 0:GCH], t.ident[rows, GCH:2 * GCH], ALU.add).then_inc(s.powers, 1)

            ssm_stages = (step_size, decay, angle, discretise, powers, chunk_step)

            def diagonal(b):
                if b:
                    dve.wait_ge(s.km_done, b)
                else:
                    dve.wait_ge(s.bbar, 1)
                    dve.wait_ge(s.bd_zero, 1)
                pairs = slice(b * BP, (b + 1) * BP)
                for g in range(2):
                    h = slice(g * NST, (g + 1) * NST)
                    link(dve.tensor_copy(t.BDr[h, :, g, :], t.Br[h, pairs, :]))
                    last = dve.tensor_scalar(t.BDi[h, :, g, :], t.Bi[h, pairs, :], -1.0, None, ALU.mult)
                    if g == 0:
                        link(last)
                last.then_inc(s.bd_ready, 1)

            def scan_block(b):
                pairs = slice(b * BP, (b + 1) * BP)
                pr, pi = t.Pr[:, pairs, :], t.Pi[:, pairs, :]
                vr, vi = (banks[6][:, c * BP * NCH:(c + 1) * BP * NCH].rearrange("p (q k) -> p q k", k=NCH) for c in range(2))
                mag8 = t.sm[:, MAG8, pairs].unsqueeze(2).broadcast_to([P, BP, NCH - 1])
                if b == 0:
                    dve.wait_ge(s.turns, N_TURNS)
                    dve.wait_ge(s.zeros_ready, 1)
                link(dve.tensor_copy(t.M8[:, :, 1:NCH], mag8))
                dve.wait_ge(s.v_done, b + 1)
                link(dve.tensor_tensor(t.vr[:], vr, pr, ALU.mult))
                link(dve.tensor_tensor(t.ta[:], vi, pi, ALU.mult))
                link(dve.tensor_tensor(t.vr[:], t.vr[:], t.ta[:], ALU.add))
                link(dve.tensor_tensor(t.vi[:], vi, pr, ALU.mult))
                link(dve.tensor_tensor(t.ta[:], vr, pi, ALU.mult))
                link(dve.tensor_tensor(t.vi[:], t.vi[:], t.ta[:], ALU.subtract))

                def flat(a):
                    return a[:].rearrange("p q k -> p (q k)")

                link(dve.tensor_tensor_scan(flat(t.ta), flat(t.M8), flat(t.vr), 0.0, ALU.mult, ALU.add))
                link(dve.tensor_tensor_scan(flat(t.tb), flat(t.M8), flat(t.vi), 0.0, ALU.mult, ALU.add))
                link(dve.tensor_tensor(t.vr[:], t.ta[:], pr, ALU.mult))
                link(dve.tensor_tensor(t.vi[:], t.tb[:], pi, ALU.mult))
                if b:
                    dve.wait_ge(s.y_done, b)
                for g in range(2):
                    h = slice(g * NST, (g + 1) * NST)
                    link(dve.tensor_tensor(t.SBr[h, :, g, 1:NCH], t.vr[h, :, 0:NCH - 1], t.vi[h, :, 0:NCH - 1], ALU.subtract))
                link(dve.tensor_tensor(t.vr[:], t.tb[:], pr, ALU.mult))
                link(dve.tensor_tensor(t.vi[:], t.ta[:], pi, ALU.mult))
                h = slice(0, NST)
                link(dve.scalar_tensor_tensor(t.SBi[h, :, 0, 1:NCH], t.vr[h, :, 0:NCH - 1], -1.0, t.vi[h, :, 0:NCH - 1],
                                              ALU.mult, ALU.subtract))
                h = slice(NST, P)
                dve.scalar_tensor_tensor(t.SBi[h, :, 1, 1:NCH], t.vr[h, :, 0:NCH - 1], -1.0, t.vi[h, :, 0:NCH - 1],
                                         ALU.mult, ALU.subtract).then_inc(s.sb_ready, 1)

            dve.memset(t.cz[:, 0:2 * NCH], 0.0).then_inc(s.cz_zero, 1)

            for kind, i in STEPS:
                if (kind, i) in TILES:
                    idx = TILES.index((kind, i))
                    ps = banks[(idx + 2) % 3]
                    lo_pro(split_for((kind, i)))
                if kind == "split":
                    lo_pro(split_for(("v", 0)))
                elif kind == "X":
                    for h in range(2):
                        g = 2 * i + h
                        dve.wait_ge(s.rows_hi, g + 1)
                        hi, lo, c = (t.memT_hi, t.memT_lo, i) if i < MT else (t.xT_hi, t.xT_lo, i - MT)
                        at = (slice(None), slice(4 * h, 4 * h + 4), slice(c * P, (c + 1) * P))
                        dve.tensor_tensor(lo[at], banks[3 + g % 3][:, :].rearrange("p (k n) -> p k n", n=P), as_f32(hi[at]),
                                          ALU.subtract).then_inc(s.rows_lo, 1)
                elif kind == "prm":
                    dve.wait_ge(s.vec_in, 9 * 16)
                    rows = slice(LDT, LDT + PAIRS)
                    dve.tensor_copy(prm[rows, :].rearrange("p (g n) -> p g n", g=2),
                                    ldt[rows, :].unsqueeze(2).broadcast_to([PAIRS, 2, NST])).then_inc(s.dt_rows, 1)
                    dve.wait_ge(s.vecs_T, 1)
                    dve.tensor_copy(t.prmT[:], banks[7][:, 0:N_VEC]).then_inc(s.vecs_cols, 1)
                elif kind == "C":
                    dve.wait_ge(s.c_T, 1)
                    dve.tensor_copy(t.CT[:].rearrange("p a q c -> p (a q c)"), banks[6][:, :]).then_inc(s.c_cols, 1)
                elif kind == "ssm":
                    ssm_stages[i]()
                    if i == len(ssm_stages) - 1:
                        diagonal(0)
                elif kind in ("k", "v", "q"):
                    dve.wait_ge(s.pro_hi, SPLIT_TILES.index((kind, i)) + 1)
                    hi, lo, at, n = {"k": (t.kT_hi, t.kT_lo, i, M), "v": (t.v_hi, t.v_lo, i, CW),
                                     "q": (t.q_hi, t.q_lo, i % 2, S)}[kind]
                    dve.tensor_tensor(lo[:, at, :], ps[:, 0:n], as_f32(hi[:, at, :]), ALU.subtract).then_inc(s.bank_out, 1)
                elif kind == "S":
                    for b in range(2):
                        dve.wait_ge(s.scores_done, 2 * i + b + 1)
                        two = slice(2 * b, 2 * b + 2)
                        if i:
                            dve.wait_ge(s.exps_done, 4 * i)
                        link(dve.tensor_reduce(rmax[:, two], banks[3 + b][:, :].rearrange("p (a m) -> p a m", m=M),
                                               axis=AX.X, op=ALU.max))
                        dve.tensor_scalar(nmax[:, two], rmax[:, two], -SCALE, None, ALU.mult).then_inc(s.neg_max, 1)
                    dve.wait_ge(s.exps_done, 4 * i + 4)
                    link(dve.reciprocal(rinv, rsum))
                    for st in range(ST):
                        last = dve.tensor_scalar(t.probs[:, st, :], t.probs[:, st, :], rinv[:, st:st + 1], None, ALU.mult)
                        if st < ST - 1:
                            link(last)
                    last.then_inc(s.probs_norm, 1)
                elif kind == "T":
                    for mt in range(MT):
                        dve.wait_ge(s.pT_hi_ready, 2 * i + mt + 1)
                        dve.tensor_tensor(t.pT_lo[:, mt, :], banks[5 + mt][:, :], as_f32(t.pT_hi[:, mt, :]),
                                          ALU.subtract).then_inc(s.pT_lo_ready, 1)
                elif kind == "O":
                    dve.wait_ge(s.o_hi_ready, i + 1)
                    dve.tensor_tensor(t.o_lo[:, i, :], banks[7][:, :], as_f32(t.o_hi[:, i, :]), ALU.subtract).then_inc(s.o_lo_ready, 1)
                elif kind == "u":
                    if i < N_TILES["u"] - 1:
                        dve.wait_ge(s.part_done, parts_before((kind, i)))
                    else:
                        dve.wait_ge(s.w_used, units_after((kind, i)))
                    dve.tensor_copy(t.uN[:, :, 3 - i, :], ps[:, :].rearrange("p (g c) -> p g c", c=GCH)).then_inc(s.bank_out, 1)
                elif kind == "KM":
                    dve.wait_ge(s.km_done, i + 1)
                    if i == 0:
                        dve.wait_ge(s.powers, 5)
                    if i:
                        dve.wait_ge(w3_in[i - 1], 2 * L * 16)
                    rows = slice(0, 2 * GCH)
                    ps = banks[5][rows, :].rearrange("p (q n) -> p q n", n=P)
                    dims = [2 * GCH, BP, GCH]
                    link(dve.tensor_tensor(t.DD[rows], t.Din[rows, i * BP:(i + 1) * BP].unsqueeze(2).broadcast_to(dims),
                                           t.patt[rows, :].unsqueeze(1).broadcast_to(dims), ALU.mult))
                    link(dve.tensor_tensor(t.Km[rows, :, 0:GCH], ps[:, :, 0:GCH], t.DD[rows], ALU.add))
                    dve.tensor_copy(t.Km[rows, :, GCH:P], ps[:, :, GCH:P]).then_inc(s.km_ready, 1)
                elif kind == "V":
                    scan_block(i)
                    if i + 1 < BLK:
                        diagonal(i + 1)
                elif kind == "YT":
                    dve.wait_ge(s.ys_hi_ready, i + 1)
                    dve.tensor_tensor(t.ys_lo[:, i, :], banks[5][:, :], as_f32(t.ys_hi[:, i, :]), ALU.subtract).then_inc(s.ys_lo_ready, 1)
                elif kind == "c":
                    ct, part, _ = conv_part(i)
                    dve.wait_ge(s.w_used, units_after((kind, i)))
                    tap = [t.prmT[:, CONVW + k * CT + ct:CONVW + k * CT + ct + 1] for k in range(3)]
                    if part == 0:
                        if ct == 0:
                            dve.wait_ge(s.o_done, HEADS)
                        dve.tensor_copy(t.cc[:], ps[:, :]).then_inc(s.bank_out, 1)
                        dve.wait_ge(s.bank_out, idx + 1)
                    elif part == 1:
                        if ct == 0:
                            dve.wait_ge(s.cz_zero, 1)
                        dve.tensor_tensor(t.cz[:, 2 * NCH:], ps[:, :], t.cc[:], ALU.mult).then_inc(s.bank_out, 1)
                        dve.wait_ge(s.bank_out, idx + 1)
                        link(dve.tensor_copy(t.cz[:, 0:2 * NCH].rearrange("p (j k) -> p j k", j=2)[:, :, 1:NCH],
                                             t.cz[:, S:S + 2 * NCH].rearrange("p (j k) -> p j k", j=2)[:, :, 0:NCH - 1]))
                        link(dve.tensor_scalar(t.cy[:], t.cz[:, 0:S], tap[0], None, ALU.mult))
                        link(dve.scalar_tensor_tensor(t.cy[:], t.cz[:, NCH:S + NCH], tap[1], t.cy[:], ALU.mult, ALU.add))
                        link(dve.scalar_tensor_tensor(t.cy[:], t.cz[:, 2 * NCH:], tap[2], t.cy[:], ALU.mult, ALU.add))
                    else:
                        dve.tensor_tensor(t.cc[:], ps[:, :], t.cy[:], ALU.mult).then_inc(s.bank_out, 1)
                        dve.wait_ge(s.bank_out, idx + 1)
                        dve.wait_ge(s.z_hi_ready, ct + 1)
                        dve.tensor_tensor(t.z_lo[:, ct, :], t.cc[:], as_f32(t.z_hi[:, ct, :]), ALU.subtract).then_inc(s.z_lo_ready, 1)
            lo_pro(N_PRO + RING)

            def merge_round(i):
                sg = t.sg
                m, v = t.mm[:, 0, :], t.mm[:, 1, :]

                def chain(k):
                    dve.wait_ge(s.merge_chain, i * 3 + k)

                dve.wait_ge(s.ya_done, i + 1)
                dve.wait_ge(s.gates_out, i * 4 + 1)
                dve.tensor_tensor(m, banks[3][:, :], sg[:, 0, :], ALU.mult).then_inc(s.bank_out, 1)
                dve.wait_ge(s.w_used, i * MIX_UNITS + (N_PRO + 4))
                dve.wait_ge(s.gates_out, i * 4 + 3)
                dve.tensor_tensor(v, banks[4][:, :], sg[:, 2, :], ALU.mult).then_inc(s.bank_out, 1)
                dve.wait_ge(s.bank_out, i * 3 + (len(TILES) + 2))
                dve.tensor_tensor(m, m, v, ALU.add).then_inc(s.merge_chain, 1)
                chain(1)
                dve.wait_ge(s.gates_out, i * 4 + 4)
                dve.tensor_tensor(v, banks[5][:, :], sg[:, 3, :], ALU.mult).then_inc(s.bank_out, 1)
                dve.wait_ge(s.bank_out, i * 3 + (len(TILES) + 3))
                dve.tensor_tensor(v, v, sg[:, 1, :], ALU.mult).then_inc(s.merged, 1)
                dve.wait_ge(s.merged, i + 1)
                dve.tensor_tensor(m, m, v, ALU.add).then_inc(s.merge_chain, 1)
                chain(2)
                hi, lo = t.m_hi[:, bass.ds(i, 1), :], t.m_lo[:, bass.ds(i, 1), :]
                m3 = t.mm[:, 0:1, :]
                dve.tensor_copy(hi, m3).then_inc(s.merge_chain, 1)
                chain(3)
                dve.tensor_tensor(lo, m3, as_f32(hi), ALU.subtract).then_inc(s.m_lo_ready, 1)
                dve.wait_ge(s.m_lo_ready, i + 1)

            def lo_unit(slot, raw_slot, count):
                dve.wait_ge(s.w_hi_ready, count)
                hi, lo = split_slot(slot)
                dve.tensor_tensor(lo, t.raw[:, raw_slot, :], as_f32(hi), ALU.subtract).then_inc(s.w_lo_ready, 1)

            with dve.Fori(0, KD - 1) as i:
                for k in range(MIX_UNITS):
                    lo_unit(k, k, i * MIX_UNITS + (N_PRO + MIX_UNITS + k + 1))
                merge_round(i)
            for k in range(RING):
                lo_unit(k, k % RAW2, OUT0 + k + 1)
            merge_round(KD - 1)
            for k in range(RING, RING2):
                lo_unit(k, k % RAW2, OUT0 + k + 1)

            def norm(n, st, gain, shift, dst, done):
                row = t.acc[:, st, :]
                for h in range(2):
                    link(dve.bn_stats(bn6[:, 6 * h:6 * h + 6], row[:, h * S:(h + 1) * S]))
                link(dve.bn_aggr(mv, bn6))
                dve.tensor_scalar(ve, mv[:, 1:2], EPS, None, ALU.add).then_inc(s.var_ready, 1)
                link(dve.scalar_tensor_tensor(dst, row, mv[:, 0:1], gain[:], ALU.subtract, ALU.mult))
                dve.wait_ge(s.sd_ready, n + 1)
                link(dve.reciprocal(ry, sd))
                link(dve.tensor_tensor(rt, ry, ry, ALU.mult))
                link(dve.tensor_tensor(rt, rt, ve, ALU.mult))
                link(dve.tensor_scalar(rt, rt, -0.5, 1.5, ALU.mult, ALU.add))
                link(dve.tensor_tensor(ry, ry, rt, ALU.mult))
                for h in range(2):
                    half = slice(h * S, (h + 1) * S)
                    dve.scalar_tensor_tensor(dst[:, half], dst[:, half], ry, shift[:, half], ALU.mult, ALU.add).then_inc(done, 1)

            def lo_x1(st):
                for h in range(2):
                    dve.wait_ge(s.x1T_hi, 2 * st + h + 1)
                    at = (slice(None), slice(4 * h, 4 * h + 4), slice(st * P, (st + 1) * P))
                    dve.tensor_tensor(t.xT_lo[at], banks[2 * st + h][:, :].rearrange("p (k n) -> p k n", n=P),
                                      as_f32(t.xT_hi[at]), ALU.subtract).then_inc(s.x1T_lo, 1)

            dve.wait_ge(s.acc_in, ST * 16)
            dve.wait_ge(s.vecs_in, 5 * 16)
            for st in range(ST):
                for dh in range(2):
                    step = 2 * st + dh
                    if st < ST - 1:
                        dve.wait_ge(s.rows_done, step + 1)
                    else:
                        dve.wait_ge(s.w_used, OUT0 + 4 * (dh + 1))
                    row = t.acc[:, st, dh * S:(dh + 1) * S]
                    dve.scalar_tensor_tensor(row, row, ALPHA, banks[step][:, :], ALU.mult, ALU.add).then_inc(s.rows_free, 1)
                if st >= 2:
                    dve.wait_ge(s.acc_ready, st - 1)
                    dve.wait_ge(s.x1_T, 2 * (st - 1))
                dve.wait_ge(s.rows_free, 2 * st + 2)
                norm(st, st, t.ln1g, t.ln1b, x1_slot(st), s.x1_ready)
                if st:
                    lo_x1(st - 1)
            for k in range(4):
                lo_unit(k, k, FF0 + k + 1)
            lo_x1(ST - 1)
            for k in range(4, 8):
                lo_unit(k, k % RAW2, FF0 + k + 1)

            dve.wait_ge(s.acc_ready, ST)

            def up_tiles(q):
                for r in range(FQ_TILES):
                    dve.wait_ge(s.sq_ready, q * FQ_TILES + (r + 1))
                    sq = t.sg[:, 2 + r % 2, :]
                    dve.tensor_copy(t.m_hi[:, r, :], sq).then_inc(s.h_hi_ready, 1)
                    dve.wait_ge(s.h_hi_ready, q * FQ_TILES + (r + 1))
                    dve.tensor_tensor(t.m_lo[:, r, :], sq, as_f32(t.m_hi[:, r, :]), ALU.subtract).then_inc(s.h_lo_ready, 1)
                    lo_unit(r, r % RAW2, q * FQ_UNITS + (FF0 + FQ_TILES + r + 1))

            def add_rows(q, step):
                st, dh = divmod(step, 2)
                if st < ST - 1:
                    dve.wait_ge(s.rows_done, q * 6 + (6 + step + 1))
                else:
                    dve.wait_ge(s.w_used, q * FQ_UNITS + (FF0 + FQ_TILES + 4 * (dh + 1)))
                row = t.acc[:, st, dh * S:(dh + 1) * S]
                dve.tensor_tensor(row, banks[step][:, :], row, ALU.add).then_inc(s.rows_free, 1)

            with dve.Fori(0, QUARTERS - 1) as q:
                up_tiles(q)
                for step in range(8):
                    add_rows(q, step)
                    if step >= 6:
                        for k in range(4):
                            u = 4 * (step - 6) + k
                            lo_unit(u, u % RAW2, q * FQ_UNITS + (FF0 + FQ_UNITS + u + 1))
            up_tiles(QUARTERS - 1)
            for st in range(ST):
                for dh in range(2):
                    add_rows(QUARTERS - 1, 2 * st + dh)
                dve.wait_ge(s.rows_free, 8 * QUARTERS + 2 * st + 2)
                norm(ST + st, st, t.ln2g, t.ln2b, t.acc[:, st, :], s.y_ready)


def kernel(x, mem, w_in, b_gate, conv_w, w_conv_out, ssm_lam_re, ssm_lam_im, ssm_log_dt, ssm_b_re, ssm_b_im,
           ssm_c_re, ssm_c_im, ssm_d, w_glu, w_kv, w_xattn_out, w_out, ln1_g, ln1_b, w_up, b_up, w_down, b_down,
           ln2_g, ln2_b):
    import concourse.bacc as bacc
    from concourse.bass_utils import run_bass_kernel_spmd

    given = dict(x=x, mem=mem, w_in=w_in, b_gate=b_gate, conv_w=conv_w, w_conv_out=w_conv_out, lam_re=ssm_lam_re,
                 lam_im=ssm_lam_im, log_dt=ssm_log_dt, b_re=ssm_b_re, b_im=ssm_b_im, c_re=ssm_c_re, c_im=ssm_c_im,
                 ssm_d=ssm_d, w_glu=w_glu, w_kv=w_kv, w_xo=w_xattn_out, w_out=w_out, ln1_g=ln1_g, ln1_b=ln1_b,
                 w_up=w_up, b_up=b_up, w_down=w_down, b_down=b_down, ln2_g=ln2_g, ln2_b=ln2_b)
    nc = bacc.Bacc("TRN2", target_bir_lowering=False, num_devices=1)
    arrays, aps = {}, {}
    for name, value in given.items():
        arrays[f"in_{name}"] = np.ascontiguousarray(value)
        aps[name] = nc.dram_tensor(f"in_{name}", value.shape, F32, kind="ExternalInput").ap()
    out = nc.dram_tensor("out", x.shape, F32, kind="ExternalOutput").ap()
    build(nc, **aps, out=out)
    result = run_bass_kernel_spmd(nc, [arrays], core_ids=[0])
    return result.results[0]["out"]
```

```python
import math
from collections import namedtuple
from contextlib import ExitStack

import numpy as np

import concourse.bass as bass
from concourse import mybir

F32 = mybir.dt.float32
F32R = mybir.dt.float32r
I32 = mybir.dt.int32
ALU = mybir.AluOpType
ACT = mybir.ActivationFunctionType
AX = mybir.AxisListType

P = 128
S = 512
D = 1024
M = 256
KD = D // P
ST = S // P
MT = M // P
CW = D // 2
CT = CW // P
HEADS = CT
GROUPS, GCH, NST = 32, 16, 64
PAIRS = GROUPS // 2
L = 8
NCH = S // L
BLK = CT
BP = PAIRS // BLK
BG = 2 * BP
UNIT = 1024
RING, RING2, RAW2 = 5, 8, 4
ALPHA = 2.0 ** 0.25
EPS = 1e-5
SCALE = float(P) ** -0.5
GATE_COLS = 3 * D
CONV_COL, U_COL, Q_COL = GATE_COLS, GATE_COLS + 3 * CW, GATE_COLS + 4 * CW

LR, LI, LDT, BGATE, BUP, CONVW = 0, 16, 32, 48, 72, 104
N_VEC = CONVW + 3 * CT

STEPS = [("X", 0), ("X", 1), ("k", 0), ("k", 1), ("X", 2), ("dt", 0), ("k", 2), ("X", 3), ("prm", 0), ("k", 3), ("X", 4),
         ("split", 0), ("X", 5), ("C", 0), ("ssm", 0), ("v", 0), ("ssm", 1), ("v", 1), ("q", 0), ("ssm", 2), ("ssm", 3),
         ("q", 1), ("S", 0), ("q", 2), ("T", 0), ("S", 1), ("q", 3), ("O", 0), ("T", 1), ("S", 2), ("u", 0), ("O", 1), ("ssm", 4),
         ("T", 2), ("S", 3), ("u", 1), ("O", 2), ("ssm", 5), ("T", 3), ("u", 2), ("ssm", 6), ("O", 3), ("u", 3), ("c", 0),
         ("UT", 0), ("UT", 1), ("UT", 2), ("UT", 3), ("QT", 0), ("KM", 0), ("V", 0), ("c", 1), ("c", 2), ("c", 3),
         ("Y", 0), ("QT", 1), ("KM", 1), ("V", 1), ("c", 4), ("YT", 0), ("c", 5),
         ("Y", 1), ("QT", 2), ("KM", 2), ("V", 2), ("c", 6), ("YT", 1), ("c", 7), ("c", 8),
         ("Y", 2), ("QT", 3), ("KM", 3), ("V", 3), ("c", 9), ("YT", 2), ("c", 10), ("Y", 3), ("c", 11), ("YT", 3)]
TILES = [s for s in STEPS if s[0] in ("k", "v", "q", "u", "c")]
SPLIT_TILES = [s for s in TILES if s[0] in ("k", "v", "q")]

PRO_UNITS = []
for _s in TILES:
    if _s in (("v", 0), ("u", 0)):
        PRO_UNITS += [(_s[0], i) for i in range(4)]
    elif _s[0] not in "vu":
        PRO_UNITS.append(_s)
UNIT_OF = {s: n for n, s in enumerate(PRO_UNITS)}
N_PRO = len(PRO_UNITS)
N_TILES = {"k": CT, "v": MT, "q": HEADS, "u": 4, "c": 3 * CT}
MIX_UNITS = 5
OUT0 = N_PRO + MIX_UNITS * KD
FF0 = OUT0 + 8
QUARTERS, FQ_TILES, FQ_UNITS = 4, 8, 16
LEAD = 4


def row_of(step):
    return 4 * (step % 2) + 3 - step // 2


def units_after(step):
    kind, i = step
    if kind in "vu":
        return UNIT_OF[kind, 0] + (4 if i == N_TILES[kind] - 1 else 0)
    return UNIT_OF[step] + 1


def split_for(step):
    kind, i = step
    if kind in "vu" and i < N_TILES[kind] - 1:
        return UNIT_OF[kind, 0] + RING
    limit = N_PRO if STEPS.index(step) < STEPS.index(("KM", BLK - 1)) else N_PRO + RING
    return min(units_after(step) + (1 if kind == "k" else LEAD), limit)


def parts_before(step):
    return len([x for x in TILES[:TILES.index(step) + 1] if x[0] in "vu" and x[1] < N_TILES[x[0]] - 1])


def conv_part(n):
    ct, part = divmod(n, 3)
    return ct, part, CONV_COL + (CW, 2 * CW, 0)[part] + ct * P

MAGIC = 1.5 * 2.0 ** 23
LOG2E = 1.0 / math.log(2.0)
LN2_HI, LN2_LO = 0.693359375, math.log(2.0) - 0.693359375
TWO_PI_1 = 6.28125
TWO_PI_2 = round((2 * math.pi - TWO_PI_1) * 2 ** 19) / 2.0 ** 19
TWO_PI_3 = 2 * math.pi - TWO_PI_1 - TWO_PI_2
ANGLE_MAX = 1.0e5
N_TURNS = 7
DT, MAG, ANG, CANG, SIN, COS, T1, T2, T3, T4, KR, KI, RDEN, MAG8, PH = range(15)
PI_BELOW = 3.1415925

def place(nc, stack, plan, found):
    room = 0
    for item in plan:
        if isinstance(item, list):
            sizes = []
            for turn in item:
                with ExitStack() as inner:
                    sizes.append(place(nc, inner, turn, found))
            stack.enter_context(nc.sbuf_tensor(f"room{len(found)}", [P, max(sizes)], F32))
            room += max(sizes)
        else:
            name, dims, dt = item
            found[name] = stack.enter_context(nc.sbuf_tensor(name, [P, *dims], dt))
            room += int(np.prod(dims))
    return room


def f32(name, *dims):
    return name, dims, F32


def hi_lo(name, *dims):
    return [(name + "_hi", dims, F32R), (name + "_lo", dims, F32R)]


def buffers(nc, stack):
    attention = hi_lo("q", 2, S) + [f32("probs", ST, M)] + hi_lo("pT", MT, S)
    block_tables = [f32("Qr", BP, L, GCH), f32("Qi", BP, L, GCH), f32("W1r", BP, P), f32("W1i", BP, P),
                    f32("W3", BG, P), f32("SBr", BP, 2, NCH), f32("SBi", BP, 2, NCH), f32("vr", BP, NCH),
                    f32("vi", BP, NCH), f32("ta", BP, NCH), f32("tb", BP, NCH), f32("cc", S), f32("cy", S)]
    ssm = [f32("Br", PAIRS, GCH), f32("Bi", PAIRS, GCH),
           f32("CT", 2, PAIRS, GCH), f32("BDr", BP, 2, GCH), f32("BDi", BP, 2, GCH),
           f32("pwr", L + 1, PAIRS), f32("pwi", L + 1, PAIRS), f32("rvr", L, PAIRS), f32("rvi", L, PAIRS), f32("sm", 18, PAIRS), ("smi", (PAIRS,), I32),
           f32("Din", PAIRS), f32("patt", GCH), f32("DD", BP, GCH), f32("Pr", PAIRS, NCH),
           f32("Pi", PAIRS, NCH), f32("M8", BP, NCH), f32("CAr", 2, BP, L + 1, GCH),
           f32("CAi", 2, BP, L + 1, GCH), f32("Km", BP, P), f32("U8", GROUPS, NCH),
           f32("Yn", L, BP, GCH), f32("cz", S + 2 * NCH), f32("pool_tmp", 2, L + 1, GCH)]
    plan = [
        f32("ident", P), f32("prmT", N_VEC), f32("small", 64),
        *hi_lo("xT", KD, S),
        f32("raw", RING, UNIT), *hi_lo("w", RING, UNIT),
        [[*hi_lo("o", CT, S), [[*hi_lo("kT", HEADS, M), *hi_lo("v", MT, CW)], hi_lo("ys", CT, S)],
          [hi_lo("memT", KD, M), [f32("uN", GROUPS, 4, GCH)], hi_lo("z", CT, S)]],
         [*hi_lo("w2", RING2 - RING, UNIT), f32("ln1g", D), f32("ln1b", D), f32("ln2g", D), f32("ln2b", D),
          f32("bdown", D)]],
        [[[[f32("xs", MT + ST, D)], attention, block_tables], *ssm],
         [*hi_lo("m", KD, S), f32("sg", 4, S), f32("mm", 2, S), f32("x1b", D), f32("acc", ST, D)]],
    ]
    found = {}
    place(nc, stack, plan, found)
    return namedtuple("Buffers", found)(**found)


SEMAPHORES = """
    ident_ready zeros_ready bd_zero cz_zero dt_rows vec_in b_in c_in d_in
    rows_T rows_hi rows_lo vecs_T vecs_cols c_T c_cols
    w_hi_ready w_lo_ready w_used part_done pro_hi bank_out
    scores_done neg_max exps_done probs_norm probs_T pT_hi_ready pT_lo_ready o_done o_hi_ready o_lo_ready
    angles sines a_ready bbar powers phases turns ca_ready q_tab bd_ready
    qt_done w1_ready km_done km_ready v_done y_done sb_ready ut_done u8_ready gelu_done yt_done ys_hi_ready ys_lo_ready
    z_hi_ready z_lo_ready
    ya_done ga_done gates_out merged merge_chain m_lo_ready
    acc_in vecs_in rows_done rows_free var_ready sd_ready x1_ready x1_T x1T_hi x1T_lo acc_ready
    up_free sq_ready h_hi_ready h_lo_ready y_ready
    dve_chain dve_stats pool_chain
""".split()


def build(nc, x, mem, w_in, b_gate, conv_w, w_conv_out, lam_re, lam_im, log_dt, b_re, b_im, c_re, c_im,
          ssm_d, w_glu, w_kv, w_xo, w_out, ln1_g, ln1_b, w_up, b_up, w_down, b_down, ln2_g, ln2_b, out):
    with ExitStack() as stack:
        t = buffers(nc, stack)
        banks = [stack.enter_context(nc.psum_tensor(f"bank{i}", [P, S], F32)) for i in range(8)]
        s = namedtuple("Semaphores", SEMAPHORES)(*[stack.enter_context(nc.semaphore(n)) for n in SEMAPHORES])

        def several(name, n):
            return [stack.enter_context(nc.semaphore(f"{name}{i}")) for i in range(n)]

        rows_in = several("rows_in", MT + ST)
        raw_pro, raw_mix, raw_late = several("raw_pro", RING), several("raw_mix", RING), several("raw_late", RAW2)
        w3_in = several("w3_in", BLK)
        out_in = several("out_in", ST)

        rmax, nmax, rsum, rinv = (t.small[:, 4 * i:4 * i + 4] for i in range(4))
        bn6 = t.small[:, 16:28]
        mv, ve, sd, ry, rt = t.small[:, 28:30], t.small[:, 30:31], t.small[:, 31:32], t.small[:, 32:33], t.small[:, 33:34]

        x_rows = x.rearrange("b (k t a) d -> (b t) a k d", t=ST, a=2)
        mem_rows = mem.rearrange("b (t p) d -> (b t) p d", p=P)
        out_rows = out.rearrange("b (k t a) d -> (b t) a k d", t=ST, a=2)
        ktiles = {k: w[0].rearrange("(t p) n -> p t n", p=P) for k, w in (
            ("in", w_in), ("kv", w_kv), ("conv", w_conv_out), ("xo", w_xo), ("glu", w_glu), ("out", w_out),
            ("up", w_up), ("down", w_down))}

        def pro_slot(n):
            return (n - N_PRO) % RING

        def split_slot(k):
            if k < RING:
                return t.w_hi[:, k, :], t.w_lo[:, k, :]
            return t.w2_hi[:, k - RING, :], t.w2_lo[:, k - RING, :]

        def tile_of(slot, i):
            hi, lo = split_slot(slot)
            return hi[:, i * P:(i + 1) * P], lo[:, i * P:(i + 1) * P]

        def half_of(slot, i):
            hi, lo = split_slot(slot)
            return hi[:, i * S:(i + 1) * S], lo[:, i * S:(i + 1) * S]

        prm = t.Yn[:, 0:2].rearrange("p j q c -> p (j q c)")
        ldt = t.Yn[:, 2, 0, 0:2]
        c_rows = t.Km

        def x1_slot(st):
            return t.mm[:].rearrange("p a n -> p (a n)") if st % 2 == 0 else t.x1b[:]

        def gate_bank(k):
            return (k + 1) % 3

        def mm3(ps, lhs, rhs, first, last):
            nc.tensor.matmul(ps, lhs[0], rhs[0], start=first, stop=False)
            nc.tensor.matmul(ps, lhs[0], rhs[1], start=False, stop=False)
            return nc.tensor.matmul(ps, lhs[1], rhs[0], start=False, stop=last)

        block = stack.enter_context(nc.Block())

        @block.sync
        def _(sp):
            def load_rows(r):
                src = mem_rows[r] if r < MT else x_rows[r - MT]
                sp.dma_start(t.xs[:, r, :], src).then_inc(rows_in[r], 16)

            def load_pro(n):
                kind, i = PRO_UNITS[n]
                if n >= RING:
                    sp.wait_ge(s.w_lo_ready, n - RING + 1)
                if kind == "v":
                    src = ktiles["kv"][:, 2 * i:2 * i + 2, CW:2 * CW]
                elif kind == "u":
                    src = ktiles["in"][:, 2 * i:2 * i + 2, U_COL:U_COL + CW]
                elif kind == "k":
                    src = ktiles["kv"][:, :, i * P:(i + 1) * P]
                else:
                    col = Q_COL + i * P if kind == "q" else conv_part(i)[2]
                    src = ktiles["in"][:, :, col:col + P]
                dst = t.raw[:, pro_slot(n), :].rearrange("p (t n) -> p t n", t=src.shape[1])
                sp.dma_start(dst, src).then_inc(raw_pro[pro_slot(n)], 16)

            load_rows(0)
            load_rows(1)
            load_pro(0)
            load_pro(1)
            load_rows(2)
            load_pro(2)
            load_rows(3)
            load_pro(3)
            load_rows(4)
            load_rows(5)
            def shift_kernel(b):
                sp.wait_ge(s.km_ready, b + 1)
                sp.wait_ge(s.zeros_ready, 1)
                if b:
                    sp.wait_ge(s.y_done, b)
                for step in range(L):
                    for g in range(2):
                        sp.dma_start(t.W3[row_of(step) * GCH:(row_of(step) + 1) * GCH, g * BP:(g + 1) * BP, step * GCH:P],
                                     t.Km[g * GCH:(g + 1) * GCH, :, 0:(L - step) * GCH]).then_inc(w3_in[b], 16)

            at = [split_for([x for x in STEPS[:STEPS.index(("KM", b))] if x in TILES][-1]) + RING - 1 for b in range(BLK)]
            blocks = 0
            for n in range(4, N_PRO):
                while blocks < BLK and at[blocks] <= n:
                    shift_kernel(blocks)
                    blocks += 1
                load_pro(n)
            for b in range(blocks, BLK):
                shift_kernel(b)
            with sp.Fori(0, KD) as i:
                for k in range(MIX_UNITS):
                    sp.wait_ge(s.w_lo_ready, i * MIX_UNITS + (N_PRO + k - RING + 1))
                    if k < 3:
                        sp.dma_start(t.raw[:, k, :].rearrange("p (t n) -> p t n", t=KD),
                                     ktiles["in"][:, :, bass.ds(i * P + k * D, P)]).then_inc(raw_mix[k], 16)
                    else:
                        parts = ((ktiles["conv"], 0), (ktiles["xo"], 0)) if k == 3 else ((ktiles["glu"], 0), (ktiles["glu"], D))
                        for h, (w, col) in enumerate(parts):
                            sp.dma_start(t.raw[:, k, h * S:(h + 1) * S].rearrange("p (t n) -> p t n", t=CT),
                                         w[:, :, bass.ds(i * P + col, P)]).then_inc(raw_mix[k], 16)
            for m in range(8):
                dh, kk = divmod(m, 4)
                sp.wait_ge(s.w_lo_ready, OUT0 + m - RAW2 + 1)
                sp.dma_start(t.raw[:, m % RAW2, :].rearrange("p (t n) -> p t n", t=2),
                             ktiles["out"][:, 2 * kk:2 * kk + 2, dh * S:(dh + 1) * S]).then_inc(raw_late[m % RAW2], 16)
            with sp.Fori(0, QUARTERS) as q:
                for r in range(FQ_UNITS):
                    sp.wait_ge(s.w_lo_ready, q * FQ_UNITS + (FF0 + r - RAW2 + 1))
                    if r < FQ_TILES:
                        sp.dma_start(t.raw[:, r % RAW2, :].rearrange("p (t n) -> p t n", t=KD),
                                     ktiles["up"][:, :, bass.ds(q * (FQ_TILES * P) + r * P, P)]).then_inc(raw_late[r % RAW2], 16)
                    else:
                        dh, kk = divmod(r - FQ_TILES, 4)
                        sp.dma_start(t.raw[:, r % RAW2, :].rearrange("p (t n) -> p t n", t=2),
                                     ktiles["down"][:, bass.ds(q * FQ_TILES + 2 * kk, 2), dh * S:(dh + 1) * S]
                                     ).then_inc(raw_late[r % RAW2], 16)
            for st in range(ST):
                for h in range(2):
                    half = slice(h * S, (h + 1) * S)
                    sp.wait_ge(s.y_ready, 2 * st + h + 1)
                    sp.dma_start(out_rows[st, :, :, half], t.acc[:, st, half]).then_inc(out_in[st], 16)
            for st in range(ST):
                sp.wait_ge(out_in[st], 2 * 16)

        @block.gpsimd
        def _(pool):
            links = [0]

            def link(ins):
                ins.then_inc(s.pool_chain, 1)
                links[0] += 1
                pool.wait_ge(s.pool_chain, links[0])

            link(pool.memset(t.ident[:], 0.0))
            pool.affine_select(out=t.ident[:], in_=t.ident[:], compare_op=ALU.not_equal, fill=1.0, base=0,
                               pattern=[[-1, P]], channel_multiplier=1).then_inc(s.ident_ready, 1)

            with nc.allow_non_contiguous_dma(reason="small per-channel vectors"):
                for g in range(2):
                    half = slice(g * NST, (g + 1) * NST)
                    pool.dma_start(prm[LR:LR + PAIRS, half], lam_re[0].rearrange("(b g q) n -> g b q n", g=2, q=BP)[g]).then_inc(s.vec_in, 16)
                    pool.dma_start(prm[LI:LI + PAIRS, half], lam_im[0].rearrange("(b g q) n -> g b q n", g=2, q=BP)[g]).then_inc(s.vec_in, 16)
                    pool.dma_start(ldt[LDT:LDT + PAIRS, g:g + 1],
                                  log_dt[0].rearrange("(b g q e) -> g b q e", g=2, q=BP, e=1)[g]).then_inc(s.vec_in, 16)
                pool.dma_start(prm[BGATE:BUP, :], b_gate[0].rearrange("(c p) -> c p", p=P)).then_inc(s.vec_in, 16)
                pool.dma_start(prm[BUP:CONVW, :], b_up[0].rearrange("(c p) -> c p", p=P)).then_inc(s.vec_in, 16)
                pool.dma_start(prm[CONVW:N_VEC, :], conv_w[0].rearrange("k (c p) -> (k c) p", p=P)).then_inc(s.vec_in, 16)
                for c, w in enumerate((c_re, c_im)):
                    rows = w[0].rearrange("(t b g q) o n -> t g b (q o) n", t=2, b=2, g=2)
                    for h in range(2):
                        for g in range(2):
                            pool.dma_start(c_rows[:, 2 * c + h, g * NST:(g + 1) * NST], rows[h, g]).then_inc(s.c_in, 16)
                for dst, w in ((t.Br, b_re), (t.Bi, b_im)):
                    for g in range(2):
                        for b in range(BLK):
                            pool.dma_start(dst[g * NST:(g + 1) * NST, b * BP:(b + 1) * BP, :],
                                          w[0].rearrange("(b g q) n c -> b g n q c", g=2, q=BP)[b, g]).then_inc(s.b_in, 16)
                for g in range(2):
                    for b in range(BLK):
                        pool.dma_start(t.Din[g * GCH:(g + 1) * GCH, b * BP:(b + 1) * BP],
                                      ssm_d[0].rearrange("(b g q c) -> b g c q", g=2, q=BP, c=GCH)[b, g]).then_inc(s.d_in, 16)

            def cmul(dr, di, ar, ai, br, bi, tmp, done):
                link(pool.tensor_tensor(dr, ar, br, ALU.mult))
                link(pool.tensor_tensor(tmp, ai, bi, ALU.mult))
                link(pool.tensor_tensor(dr, dr, tmp, ALU.subtract))
                link(pool.tensor_tensor(di, ar, bi, ALU.mult))
                link(pool.tensor_tensor(tmp, ai, br, ALU.mult))
                pool.tensor_tensor(di, di, tmp, ALU.add).then_inc(done, 1)

            def c_powers(b):
                if b >= 2:
                    pool.wait_ge(s.y_done, b - 1)
                for h in range(2):
                    if b or h:
                        pool.wait_ge(s.ca_ready, 2 * b + h)
                    pairs = slice(b * BP + 2 * h, b * BP + 2 * h + 2)
                    dims = [P, 2, L + 1, GCH]
                    ar = t.pwr[:].rearrange("p l q -> p q l")[:, pairs, :].unsqueeze(3).broadcast_to(dims)
                    ai = t.pwi[:].rearrange("p l q -> p q l")[:, pairs, :].unsqueeze(3).broadcast_to(dims)
                    cr = t.CT[:, 0, pairs, :].unsqueeze(2).broadcast_to(dims)
                    ci = t.CT[:, 1, pairs, :].unsqueeze(2).broadcast_to(dims)
                    cmul(t.CAr[:, b % 2, 2 * h:2 * h + 2], t.CAi[:, b % 2, 2 * h:2 * h + 2], ar, ai, cr, ci,
                         t.pool_tmp[:], s.ca_ready)

            def input_powers(b):
                if b:
                    pool.wait_ge(s.qt_done, 2 * b)
                for h in range(2):
                    pairs = slice(b * BP + 2 * h, b * BP + 2 * h + 2)
                    dims = [P, 2, L, GCH]
                    ar = t.rvr[:].rearrange("p l q -> p q l")[:, pairs, :].unsqueeze(3).broadcast_to(dims)
                    ai = t.rvi[:].rearrange("p l q -> p q l")[:, pairs, :].unsqueeze(3).broadcast_to(dims)
                    br = t.Br[:, pairs, :].unsqueeze(2).broadcast_to(dims)
                    bi = t.Bi[:, pairs, :].unsqueeze(2).broadcast_to(dims)
                    pool.wait_ge(s.ca_ready, 2 * b + 2)
                    if b or h:
                        pool.wait_ge(s.q_tab, 2 * b + h)
                    cmul(t.Qr[:, 2 * h:2 * h + 2], t.Qi[:, 2 * h:2 * h + 2], ar, ai, br, bi,
                         t.pool_tmp[:, :, 0:L, :], s.q_tab)

            link(pool.memset(t.pwr[:, 0, :], 1.0))
            link(pool.memset(t.pwi[:, 0, :], 0.0))
            link(pool.memset(t.BDr[:], 0.0))
            link(pool.memset(t.BDi[:], 0.0))
            link(pool.memset(t.M8[:], 0.0))
            link(pool.memset(t.Pr[:, :, 0], 1.0))
            pool.memset(t.Pi[:, :, 0], 0.0).then_inc(s.bd_zero, 1)
            pool.wait_ge(s.c_cols, 1)
            pool.wait_ge(s.a_ready, 1)
            flat_tmp = t.pool_tmp[:].rearrange("p a l c -> p (a l c)")

            def tmp_of(*dims):
                n = int(np.prod(dims))
                return flat_tmp[:, 0:n] if len(dims) == 1 else flat_tmp[:, 0:n].rearrange("p (a b) -> p a b", b=dims[1])

            m = 1
            while m < L:
                dims = [P, m, PAIRS]
                cmul(t.pwr[:, m + 1:2 * m + 1, :], t.pwi[:, m + 1:2 * m + 1, :], t.pwr[:, 1:m + 1, :], t.pwi[:, 1:m + 1, :],
                     t.pwr[:, m:m + 1, :].broadcast_to(dims), t.pwi[:, m:m + 1, :].broadcast_to(dims), tmp_of(m, PAIRS), s.powers)
                m *= 2
                pool.wait_ge(s.powers, m.bit_length() - 1)
            for dst, src in ((t.rvr, t.pwr), (t.rvi, t.pwi)):
                link(pool.tensor_copy(dst[:, 0:4, :], src[:, 1:8:2, :]))
                link(pool.tensor_copy(dst[:, 4:8, :], src[:, 0:7:2, :]))
            c_powers(0)
            pool.wait_ge(s.ca_ready, 2)
            pr, pi = t.sm[:, COS, :], t.sm[:, SIN, :]
            for k in range(3):
                dr, di = (t.Pr[:, :, 1], t.Pi[:, :, 1]) if k == 2 else (t.sm[:, PH + 2 * k, :], t.sm[:, PH + 2 * k + 1, :])
                cmul(dr, di, pr, pi, pr, pi, tmp_of(PAIRS), s.phases)
                pool.wait_ge(s.phases, k + 1)
                pr, pi = dr, di
            m, n_turns = 1, 0
            while m < NCH - 1:
                n = min(m, NCH - 1 - m)
                parts = -(-PAIRS * n // flat_tmp.shape[1])
                for h in range(parts):
                    half = slice(h * PAIRS // parts, (h + 1) * PAIRS // parts)
                    dims = [P, PAIRS // parts, n]
                    cmul(t.Pr[:, half, m + 1:m + 1 + n], t.Pi[:, half, m + 1:m + 1 + n],
                         t.Pr[:, half, 1:1 + n], t.Pi[:, half, 1:1 + n],
                         t.Pr[:, half, m:m + 1].broadcast_to(dims), t.Pi[:, half, m:m + 1].broadcast_to(dims),
                         tmp_of(*dims[1:]), s.turns)
                    n_turns += 1
                    pool.wait_ge(s.turns, n_turns)
                m += n
            assert n_turns == N_TURNS
            pool.wait_ge(s.o_done, HEADS)
            pool.wait_ge(s.bbar, 1)
            for b in range(BLK):
                input_powers(b)
                if b == 0:
                    link(pool.memset(t.W3[:], 0.0))
                    link(pool.memset(t.SBr[:], 0.0))
                    pool.memset(t.SBi[:], 0.0).then_inc(s.zeros_ready, 1)
                if b + 1 < BLK:
                    pool.wait_ge(s.q_tab, 2 * b + 2)
                    c_powers(b + 1)
            pool.wait_ge(s.ys_lo_ready, BLK)
            for st in range(ST):
                pool.dma_start(t.acc[:, st, :], x_rows[st]).then_inc(s.acc_in, 16)
            pool.wait_ge(s.w_used, OUT0)
            for dst, src in ((t.ln1g, ln1_g), (t.ln1b, ln1_b), (t.bdown, b_down), (t.ln2g, ln2_g), (t.ln2b, ln2_b)):
                pool.dma_start(dst[:], src[0].partition_broadcast(P)).then_inc(s.vecs_in, 16)
            pool.wait_ge(s.vecs_in, 5 * 16)
            for st in range(ST):
                pool.wait_ge(s.x1_ready, 2 * st + 2)
                link(pool.tensor_scalar(t.acc[:, st, :], x1_slot(st), ALPHA, None, ALU.mult))
                pool.tensor_tensor(t.acc[:, st, :], t.acc[:, st, :], t.bdown[:], ALU.add).then_inc(s.acc_ready, 1)

        @block.tensor
        def _(pe):
            def weights(n):
                pe.wait_ge(s.w_lo_ready, n + 1)

            def turn(out, rows, h):
                return pe.matmul(out, rows, t.ident[h, h], start=True, stop=True)

            pe.wait_ge(s.ident_ready, 1)
            for kind, i in STEPS:
                if kind in ("k", "v", "q", "u", "c"):
                    idx = TILES.index((kind, i))
                    ps = banks[(idx + 2) % 3]
                    if idx >= 3:
                        pe.wait_ge(s.bank_out, idx - 2)
                if kind == "X":
                    pe.wait_ge(rows_in[i], 16)
                    for h in range(2):
                        g = 2 * i + h
                        if g >= 3:
                            pe.wait_ge(s.rows_lo, g - 2)
                        for k in range(4):
                            kt = 4 * h + k
                            last = pe.transpose(banks[3 + g % 3][:, k * P:(k + 1) * P], t.xs[:, i, kt * P:(kt + 1) * P], t.ident[:])
                        last.then_inc(s.rows_T, 1)
                elif kind == "prm":
                    pe.wait_ge(s.dt_rows, 1)
                    pe.transpose(banks[7][:, 0:N_VEC], prm[0:N_VEC, :], t.ident[0:N_VEC, 0:N_VEC]).then_inc(s.vecs_T, 1)
                elif kind == "C":
                    pe.wait_ge(s.c_in, 8 * 16)
                    for k in range(4):
                        last = pe.transpose(banks[6][:, k * P:(k + 1) * P], c_rows[:, k, :], t.ident[:])
                    last.then_inc(s.c_T, 1)
                elif kind == "k":
                    weights(UNIT_OF[kind, i])
                    pe.wait_ge(s.rows_lo, 2 * MT)
                    for kt in range(KD):
                        last = mm3(ps[:, 0:M], tile_of(pro_slot(UNIT_OF[kind, i]), kt),
                                   (t.memT_hi[:, kt, :], t.memT_lo[:, kt, :]), kt == 0, kt == KD - 1)
                    last.then_inc(s.w_used, 1)
                elif kind in ("v", "u"):
                    if kind == "u":
                        pe.wait_ge(s.rows_lo, 2 * (MT + ST))
                    for kt in range(KD):
                        n = UNIT_OF[kind, 0] + kt // 2
                        weights(n)
                        if kind == "v":
                            rows = [a[:, kt, i * P:(i + 1) * P] for a in (t.memT_hi, t.memT_lo)]
                        else:
                            rows = [a[:, kt, i * P:(i + 1) * P] for a in (t.xT_hi, t.xT_lo)]
                        last = mm3(ps[:, :], rows, half_of(pro_slot(n), kt % 2), kt == 0, kt == KD - 1)
                        if i == N_TILES[kind] - 1 and kt % 2:
                            last.then_inc(s.w_used, 1)
                    if i < N_TILES[kind] - 1:
                        last.then_inc(s.part_done, 1)
                elif kind in ("q", "c"):
                    weights(UNIT_OF[kind, i])
                    pe.wait_ge(s.rows_lo, 2 * (MT + ST))
                    for kt in range(KD):
                        last = mm3(ps[:, :], tile_of(pro_slot(UNIT_OF[kind, i]), kt),
                                   (t.xT_hi[:, kt, :], t.xT_lo[:, kt, :]), kt == 0, kt == KD - 1)
                    last.then_inc(s.w_used, 1)
                elif kind == "S":
                    pe.wait_ge(s.bank_out, TILES.index(("q", i)) + 1)
                    if i:
                        pe.wait_ge(s.exps_done, 4 * i)
                    for st in range(ST):
                        q = [a[:, i % 2, st * P:(st + 1) * P] for a in (t.q_hi, t.q_lo)]
                        last = mm3(banks[3 + st // 2][:, (st % 2) * M:(st % 2 + 1) * M], q,
                                   (t.kT_hi[:, i, :], t.kT_lo[:, i, :]), True, True)
                        if st % 2:
                            last.then_inc(s.scores_done, 1)
                elif kind == "T":
                    pe.wait_ge(s.probs_norm, i + 1)
                    if i:
                        pe.wait_ge(s.pT_lo_ready, 2 * i)
                    for mt in range(MT):
                        for st in range(ST):
                            last = pe.transpose(banks[5 + mt][:, st * P:(st + 1) * P], t.probs[:, st, mt * P:(mt + 1) * P], t.ident[:])
                        last.then_inc(s.probs_T, 1)
                elif kind == "O":
                    pe.wait_ge(s.pT_lo_ready, 2 * i + 2)
                    if i:
                        pe.wait_ge(s.o_lo_ready, i)
                    for mt in range(MT):
                        v = [a[:, mt, i * P:(i + 1) * P] for a in (t.v_hi, t.v_lo)]
                        last = mm3(banks[7][:, :], v, (t.pT_hi[:, mt, :], t.pT_lo[:, mt, :]), mt == 0, mt == MT - 1)
                    last.then_inc(s.o_done, 1)
                elif kind == "UT":
                    pe.wait_ge(s.bank_out, TILES.index(("u", 3)) + 1)
                    for g in range(BG):
                        for a in range(2):
                            h = slice(a * NCH, (a + 1) * NCH)
                            last = turn(banks[3 + i][h, g * NCH:(g + 1) * NCH], t.uN[h, i * BG + g].rearrange("p l c -> p (l c)"), h)
                    last.then_inc(s.ut_done, 1)
                elif kind == "YT":
                    pe.wait_ge(s.gelu_done, i + 1)
                    pe.wait_ge(s.km_ready, min(i + 2, BLK))
                    if i:
                        pe.wait_ge(s.ys_lo_ready, i)
                    for j in range(L):
                        for g in range(2):
                            h = slice(g * NCH, (g + 1) * NCH)
                            last = turn(banks[5][h, j * NCH:(j + 1) * NCH], t.Yn[h, j].rearrange("p q c -> p (q c)"), h)
                    last.then_inc(s.yt_done, 1)
                elif kind == "QT":
                    pe.wait_ge(s.q_tab, 2 * i + 2)
                    if i == 0:
                        pe.wait_ge(s.u8_ready, 2)
                    if i:
                        pe.wait_ge(s.w1_ready, 2 * i)
                    for c, tab in enumerate((t.Qr, t.Qi)):
                        for q in range(BP):
                            last = pe.transpose(banks[3 + c][:, q * P:(q + 1) * P],
                                                tab[:, q].rearrange("p l c -> p (l c)"), t.ident[:])
                        last.then_inc(s.qt_done, 1)
                elif kind == "KM":
                    pe.wait_ge(s.bd_ready, i + 1)
                    pe.wait_ge(s.ca_ready, 2 * i + 2)
                    if i == 0:
                        pe.wait_ge(s.u8_ready, BLK)
                    if i:
                        pe.wait_ge(s.km_ready, i)
                    if i >= 2:
                        pe.wait_ge(s.ys_lo_ready, i - 1)
                    for q in range(BP):
                        ca = [a[:, i % 2, q, 0:L, :].rearrange("p l c -> p (l c)") for a in (t.CAr, t.CAi)]
                        pe.matmul(banks[5][0:2 * GCH, q * P:(q + 1) * P], t.BDr[:, q].rearrange("p g c -> p (g c)"), ca[0],
                                  start=True, stop=False)
                        last = pe.matmul(banks[5][0:2 * GCH, q * P:(q + 1) * P], t.BDi[:, q].rearrange("p g c -> p (g c)"), ca[1],
                                         start=False, stop=True)
                    last.then_inc(s.km_done, 1)
                elif kind == "V":
                    pe.wait_ge(s.w1_ready, 2 * i + 2)
                    pe.wait_ge(s.u8_ready, i + 1)
                    if i:
                        pe.wait_ge(s.sb_ready, i)
                    for q in range(BP):
                        for g in range(2):
                            half = slice(g * NST, (g + 1) * NST)
                            for c, w in enumerate((t.W1r, t.W1i)):
                                last = pe.matmul(banks[6][half, c * BP * NCH + q * NCH:c * BP * NCH + (q + 1) * NCH],
                                                 w[:, q, half], t.U8[:, i * BG + g * BP + q, :], start=True, stop=True)
                    last.then_inc(s.v_done, 1)
                elif kind == "Y":
                    pe.wait_ge(s.sb_ready, i + 1)
                    pe.wait_ge(w3_in[i], 2 * L * 16)
                    if i:
                        pe.wait_ge(s.gelu_done, i)
                    for q in range(BP):
                        ps = banks[7][:, q * P:(q + 1) * P]
                        ca = [a[:, i % 2, q, 1:L + 1, :].rearrange("p l c -> p (l c)") for a in (t.CAr, t.CAi)]
                        pe.matmul(ps, t.SBr[:, q].rearrange("p g k -> p (g k)"), ca[0], start=True, stop=False)
                        pe.matmul(ps, t.SBi[:, q].rearrange("p g k -> p (g k)"), ca[1], start=False, stop=False)
                        for g in range(2):
                            last = pe.matmul(banks[7][g * NCH:(g + 1) * NCH, q * P:(q + 1) * P], t.U8[:, i * BG + g * BP + q, :],
                                             t.W3[:, g * BP + q, :], start=False, stop=True)
                    last.then_inc(s.y_done, 1)

            pe.wait_ge(s.bank_out, len(TILES) - 1)
            with pe.Fori(0, KD) as i:
                for k in range(MIX_UNITS):
                    pe.wait_ge(s.w_lo_ready, i * MIX_UNITS + (N_PRO + k + 1))
                    if k < 3:
                        if k == 2:
                            pe.wait_ge(s.bank_out, i * 3 + len(TILES))
                        for kt in range(KD):
                            last = mm3(banks[gate_bank(k)][:, :], tile_of(k, kt), (t.xT_hi[:, kt, :], t.xT_lo[:, kt, :]), kt == 0, kt == KD - 1)
                        last.then_inc(s.w_used, 1)
                        continue
                    for h in range(2):
                        bank = 3 + 2 * (k - 3) + h
                        if k == 3 and h == 0:
                            pe.wait_ge(s.z_lo_ready, CT)
                            src = (t.z_hi, t.z_lo)
                        elif k == 3:
                            pe.wait_ge(s.o_lo_ready, HEADS)
                            src = (t.o_hi, t.o_lo)
                        else:
                            pe.wait_ge(s.ys_lo_ready, BLK)
                            src = (t.ys_hi, t.ys_lo)
                        for kt in range(CT):
                            last = mm3(banks[bank][:, :], tile_of(k, h * CT + kt), (src[0][:, kt, :], src[1][:, kt, :]), kt == 0, kt == CT - 1)
                        last.then_inc(s.w_used if h else (s.ya_done, s.ga_done)[k - 3], 1)

            def transpose_x1(st):
                for h in range(2):
                    pe.wait_ge(s.x1_ready, 2 * st + h + 1)
                    for k in range(4):
                        kt = 4 * h + k
                        last = pe.transpose(banks[2 * st + h][:, k * P:(k + 1) * P], x1_slot(st)[:, kt * P:(kt + 1) * P], t.ident[:])
                    last.then_inc(s.x1_T, 1)

            def row_step(st, dh, kts):
                for kt in kts:
                    last = mm3(banks[2 * st + dh][:, :], (t.m_hi[:, kt, st * P:(st + 1) * P], t.m_lo[:, kt, st * P:(st + 1) * P]),
                               half_of(4 * dh + kt // 2, kt % 2), kt == 0, kt == KD - 1)
                    if st == ST - 1 and kt % 2:
                        last.then_inc(s.w_used, 1)
                if st < ST - 1 and kts[-1] == KD - 1:
                    last.then_inc(s.rows_done, 1)

            pe.wait_ge(s.gates_out, 4 * (KD - 1) + 3)
            for st in range(2):
                for kt in range(KD - 1):
                    if st == 0:
                        pe.wait_ge(s.w_lo_ready, OUT0 + kt // 2 + 1)
                        pe.wait_ge(s.m_lo_ready, kt + 1)
                    row_step(st, 0, [kt])
            pe.wait_ge(s.m_lo_ready, KD)
            for st in range(2):
                row_step(st, 0, [KD - 1])
            for kt in range(KD):
                pe.wait_ge(s.w_lo_ready, OUT0 + 4 + kt // 2 + 1)
                row_step(0, 1, [kt])
            pe.wait_ge(s.bank_out, len(TILES) + 3 * KD)
            pe.wait_ge(s.gates_out, 4 * KD)
            row_step(1, 1, range(KD))
            for st in range(2, ST):
                for dh in range(2):
                    row_step(st, dh, range(KD))
                    if st == 2:
                        transpose_x1(dh)
            transpose_x1(2)

            def up_tile(r, cols):
                for kt in range(KD):
                    last = mm3(banks[r][:, cols], tile_of(r, kt), (t.xT_hi[:, kt, cols], t.xT_lo[:, kt, cols]), kt == 0, kt == KD - 1)
                return last

            half = S // 2
            pe.wait_ge(s.x1T_lo, 4)
            for r in range(FQ_TILES // 2):
                pe.wait_ge(s.w_lo_ready, FF0 + r + 1)
                up_tile(r, slice(0, half))
                if r == 1:
                    transpose_x1(ST - 1)
            pe.wait_ge(s.x1T_lo, 2 * ST)
            for r in range(FQ_TILES):
                if r < FQ_TILES // 2:
                    last = up_tile(r, slice(half, S))
                else:
                    pe.wait_ge(s.w_lo_ready, FF0 + r + 1)
                    last = up_tile(r, slice(0, S))
                last.then_inc(s.w_used, 1)

            def down(q):
                for step in range(8):
                    st, dh = divmod(step, 2)
                    pe.wait_ge(s.up_free, q * FQ_TILES + (step + 1))
                    for kt in range(KD):
                        if st == 0 and kt % 2 == 0:
                            pe.wait_ge(s.w_lo_ready, q * FQ_UNITS + (FF0 + FQ_TILES + 4 * dh + kt // 2 + 1))
                        if step == 0:
                            pe.wait_ge(s.h_lo_ready, q * FQ_TILES + (kt + 1))
                        row_step(st, dh, [kt])

            with pe.Fori(0, QUARTERS - 1) as q:
                down(q)
                for r in range(FQ_TILES):
                    pe.wait_ge(s.w_lo_ready, q * FQ_UNITS + (FF0 + FQ_UNITS + r + 1))
                    pe.wait_ge(s.rows_free, q * 8 + (8 + r + 1))
                    up_tile(r, slice(0, S)).then_inc(s.w_used, 1)
            down(QUARTERS - 1)

        @block.scalar
        def _(act):
            split_to = [0]

            def hi_pro(upto):
                while split_to[0] < upto:
                    n = split_to[0]
                    slot = pro_slot(n)
                    act.wait_ge((raw_pro if n < N_PRO else raw_mix)[slot],
                                16 * (n // RING + 1) if n < N_PRO else (16 if slot < 3 else 32))
                    if n >= RING:
                        act.wait_ge(s.w_used, n - RING + 1)
                    act.activation(split_slot(slot)[0], t.raw[:, slot, :], ACT.Copy).then_inc(s.w_hi_ready, 1)
                    split_to[0] += 1

            for kind, i in STEPS:
                if (kind, i) in TILES:
                    hi_pro(split_for((kind, i)))
                if kind == "split":
                    hi_pro(split_for(("v", 0)))
                if kind == "X":
                    for h in range(2):
                        g = 2 * i + h
                        act.wait_ge(s.rows_T, g + 1)
                        dst = (t.memT_hi[:, 4 * h:4 * h + 4, i * P:(i + 1) * P] if i < MT else
                               t.xT_hi[:, 4 * h:4 * h + 4, (i - MT) * P:(i - MT + 1) * P])
                        act.activation(dst, banks[3 + g % 3][:, :].rearrange("p (k n) -> p k n", n=P), ACT.Copy).then_inc(s.rows_hi, 1)
                elif (kind, i) == ("ssm", 2):
                    act.wait_ge(s.angles, 1)
                    act.activation(t.sm[:, SIN, :], t.sm[:, ANG, :], ACT.Sin).then_inc(s.sines, 1)
                    act.activation(t.sm[:, COS, :], t.sm[:, CANG, :], ACT.Sin).then_inc(s.sines, 1)
                elif kind in ("k", "v", "q"):
                    idx = TILES.index((kind, i))
                    ps = banks[(idx + 2) % 3]
                    if (kind, i) == ("v", 0):
                        act.wait_ge(s.part_done, 1)
                    else:
                        act.wait_ge(s.w_used, units_after((kind, i)))
                    if kind == "k":
                        act.activation(t.kT_hi[:, i, :], ps[:, 0:M], ACT.Copy).then_inc(s.pro_hi, 1)
                    elif kind == "v":
                        act.activation(t.v_hi[:, i, :], ps[:, :], ACT.Copy).then_inc(s.pro_hi, 1)
                    else:
                        if i == 0:
                            act.wait_ge(s.rows_T, 2 * (MT + ST))
                        if i >= 2:
                            act.wait_ge(s.scores_done, 2 * (i - 1))
                        act.activation(t.q_hi[:, i % 2, :], ps[:, :], ACT.Copy).then_inc(s.pro_hi, 1)
                elif kind == "S":
                    if i:
                        act.wait_ge(s.probs_T, 2 * i)
                    for st in range(ST):
                        act.wait_ge(s.neg_max, 2 * i + st // 2 + 1)
                        act.activation(t.probs[:, st, :], banks[3 + st // 2][:, (st % 2) * M:(st % 2 + 1) * M], ACT.Exp,
                                       bias=nmax[:, st:st + 1], scale=SCALE, accum_out=rsum[:, st:st + 1]).then_inc(s.exps_done, 1)
                elif kind == "T":
                    for mt in range(MT):
                        act.wait_ge(s.probs_T, 2 * i + mt + 1)
                        if i and mt == 0:
                            act.wait_ge(s.o_done, i)
                        act.activation(t.pT_hi[:, mt, :], banks[5 + mt][:, :], ACT.Copy).then_inc(s.pT_hi_ready, 1)
                elif kind == "O":
                    act.wait_ge(s.o_done, i + 1)
                    act.activation(t.o_hi[:, i, :], banks[7][:, :], ACT.Copy).then_inc(s.o_hi_ready, 1)
                elif kind == "UT":
                    act.wait_ge(s.ut_done, i + 1)
                    act.activation(t.U8[:, i * BG:(i + 1) * BG, :].rearrange("p g k -> p (g k)"), banks[3 + i][:, :],
                                   ACT.Copy).then_inc(s.u8_ready, 1)
                elif kind == "QT":
                    for c, dst in enumerate((t.W1r, t.W1i)):
                        act.wait_ge(s.qt_done, 2 * i + c + 1)
                        act.activation(dst[:].rearrange("p q n -> p (q n)"), banks[3 + c][:, :], ACT.Copy).then_inc(s.w1_ready, 1)
                elif kind == "Y":
                    act.wait_ge(s.y_done, i + 1)
                    if i:
                        act.wait_ge(s.yt_done, i)
                    act.activation(t.Yn[:].rearrange("p j q c -> p q j c"), banks[7][:, :].rearrange("p (q j c) -> p q j c", q=BP, c=GCH),
                                   ACT.Gelu_apprx_tanh).then_inc(s.gelu_done, 1)
                elif kind == "YT":
                    act.wait_ge(s.yt_done, i + 1)
                    act.activation(t.ys_hi[:, i, :], banks[5][:, :], ACT.Copy).then_inc(s.ys_hi_ready, 1)
                elif kind == "c" and i % 3 == 2:
                    act.wait_ge(s.bank_out, TILES.index((kind, i)) + 1)
                    act.activation(t.z_hi[:, i // 3, :], t.cc[:], ACT.Copy).then_inc(s.z_hi_ready, 1)
            hi_pro(N_PRO + RING)

            act.wait_ge(s.ys_lo_ready, BLK)

            def merge_round(i, split_next):
                for k in range(MIX_UNITS):
                    if k < 3 or k == 4:
                        sg = min(k, 3)
                        bank = gate_bank(k) if k < 3 else 6
                        act.wait_ge(s.w_used, i * MIX_UNITS + (N_PRO + k + 1))
                        if k < 3:
                            act.activation(t.sg[:, sg, :], banks[bank][:, :], ACT.Sigmoid,
                                           bias=t.prmT[:, bass.ds(i + (BGATE + k * KD), 1)]).then_inc(s.gates_out, 1)
                        else:
                            act.activation(t.sg[:, sg, :], banks[bank][:, :], ACT.Sigmoid).then_inc(s.gates_out, 1)
                    split_next(k)
                act.wait_ge(s.merged, i + 1)

            with act.Fori(0, KD - 1) as i:
                def hi_mix(k):
                    act.wait_ge(raw_mix[k], i * (16 if k < 3 else 32) + (32 if k < 3 else 64))
                    act.wait_ge(s.w_used, i * MIX_UNITS + (N_PRO + k + 1))
                    act.activation(split_slot(k)[0], t.raw[:, k, :], ACT.Copy).then_inc(s.w_hi_ready, 1)
                merge_round(i, hi_mix)

            def hi_late(m, slot, count, used):
                act.wait_ge(raw_late[m % RAW2], count)
                act.wait_ge(s.w_used, used)
                act.activation(split_slot(slot)[0], t.raw[:, m % RAW2, :], ACT.Copy).then_inc(s.w_hi_ready, 1)

            merge_round(KD - 1, lambda k: hi_late(k, k, 16 * (k // RAW2 + 1), OUT0 - MIX_UNITS + k + 1))
            for k in range(RING, RING2):
                hi_late(k, k, 16 * (k // RAW2 + 1), OUT0)

            def sqrt_var(n):
                act.wait_ge(s.var_ready, n + 1)
                act.activation(sd, ve, ACT.Sqrt).then_inc(s.sd_ready, 1)

            def hi_x1(st):
                for h in range(2):
                    act.wait_ge(s.x1_T, 2 * st + h + 1)
                    act.activation(t.xT_hi[:, 4 * h:4 * h + 4, st * P:(st + 1) * P],
                                   banks[2 * st + h][:, :].rearrange("p (k n) -> p k n", n=P), ACT.Copy).then_inc(s.x1T_hi, 1)

            sqrt_var(0)
            sqrt_var(1)
            hi_x1(0)
            hi_x1(1)
            sqrt_var(2)
            for k in range(4):
                hi_late(8 + k, k, 16 * ((8 + k) // RAW2 + 1), OUT0 + k + 1)
            hi_x1(2)
            sqrt_var(3)
            hi_x1(3)
            for k in range(4, 8):
                hi_late(8 + k, k, 16 * ((8 + k) // RAW2 + 1), OUT0 + k + 1)

            def quarter(q, last):
                for r in range(FQ_TILES):
                    act.wait_ge(s.w_used, q * FQ_UNITS + (FF0 + r + 1))
                    if r >= 2:
                        act.wait_ge(s.h_lo_ready, q * FQ_TILES + (r - 1))
                    act.activation(t.sg[:, r % 2, :], banks[r][:, :], ACT.Relu,
                                   bias=t.prmT[:, bass.ds(q * FQ_TILES + (BUP + r), 1)]).then_inc(s.up_free, 1)
                    act.wait_ge(s.up_free, q * FQ_TILES + (r + 1))
                    act.activation(t.sg[:, 2 + r % 2, :], t.sg[:, r % 2, :], ACT.Square).then_inc(s.sq_ready, 1)
                    hi_late(r, r, q * (16 * FQ_UNITS // RAW2) + 16 * ((16 + r) // RAW2 + 1), q * FQ_UNITS + (FF0 + r + 1))
                if not last:
                    act.wait_ge(s.h_lo_ready, q * FQ_TILES + FQ_TILES)
                    for k in range(8):
                        hi_late(k, k, q * (16 * FQ_UNITS // RAW2) + 16 * ((24 + k) // RAW2 + 1),
                                q * FQ_UNITS + (FF0 + FQ_TILES + k + 1))

            with act.Fori(0, QUARTERS - 1) as q:
                quarter(q, False)
            quarter(QUARTERS - 1, True)
            for st in range(ST):
                sqrt_var(ST + st)

        @block.vector
        def _(dve):
            links = [0]
            split_to = [0]

            def link(ins):
                ins.then_inc(s.dve_chain, 1)
                links[0] += 1
                dve.wait_ge(s.dve_chain, links[0])

            def as_f32(ap):
                return ap.bitcast(F32)

            def lo_pro(upto):
                while split_to[0] < upto:
                    n = split_to[0]
                    slot = pro_slot(n)
                    dve.wait_ge(s.w_hi_ready, n + 1)
                    hi, lo = split_slot(slot)
                    dve.tensor_tensor(lo, t.raw[:, slot, :], as_f32(hi), ALU.subtract).then_inc(s.w_lo_ready, 1)
                    split_to[0] += 1

            def sm(i):
                return t.sm[:, i, :]

            def vexp(dst, src):
                c, n, r, bits = sm(T1), sm(T2), sm(T3), t.smi[:]
                link(dve.tensor_scalar(c, src, -104.0, 89.0, ALU.max, ALU.min))
                link(dve.tensor_scalar(n, c, LOG2E, MAGIC, ALU.mult, ALU.add))
                link(dve.tensor_scalar(n, n, MAGIC, None, ALU.subtract))
                link(dve.scalar_tensor_tensor(r, n, -LN2_HI, c, ALU.mult, ALU.add))
                link(dve.scalar_tensor_tensor(r, n, -LN2_LO, r, ALU.mult, ALU.add))
                link(dve.tensor_scalar(n, n, -127.0, 128.0, ALU.max, ALU.min))
                link(dve.tensor_scalar(bits, n, 127.0, None, ALU.add))
                link(dve.tensor_scalar(bits, bits, 23, None, ALU.logical_shift_left))
                link(dve.tensor_scalar(c, r, 1.0 / math.factorial(7), None, ALU.mult))
                for k in (6, 5, 4, 3, 2, 1):
                    link(dve.scalar_tensor_tensor(c, c, 1.0 / math.factorial(k), r, ALU.add, ALU.mult))
                link(dve.scalar_tensor_tensor(dst, c, 1.0, bits.bitcast(F32), ALU.add, ALU.mult))

            lr, li, ld = (t.prmT[:, c:c + PAIRS] for c in (LR, LI, LDT))
            tmp = t.U8[:, 0:16, :].rearrange("p g k -> p (g k)").rearrange("p (n q c) -> p n q c", n=4, c=GCH)

            def step_size():
                dve.wait_ge(s.vecs_cols, 1)
                vexp(sm(DT), ld)

            def decay():
                link(dve.tensor_tensor(sm(T4), lr, sm(DT), ALU.mult))
                vexp(sm(MAG), sm(T4))

            def angle():
                link(dve.tensor_tensor(sm(ANG), li, sm(DT), ALU.mult))
                link(dve.tensor_scalar(sm(ANG), sm(ANG), -ANGLE_MAX, ANGLE_MAX, ALU.max, ALU.min))
                link(dve.tensor_scalar(sm(T1), sm(ANG), 1.0 / (2 * math.pi), MAGIC, ALU.mult, ALU.add))
                link(dve.tensor_scalar(sm(T1), sm(T1), MAGIC, None, ALU.subtract))
                for part in (TWO_PI_1, TWO_PI_2, TWO_PI_3):
                    link(dve.scalar_tensor_tensor(sm(ANG), sm(T1), -part, sm(ANG), ALU.mult, ALU.add))
                link(dve.tensor_scalar(sm(ANG), sm(ANG), -PI_BELOW, PI_BELOW, ALU.max, ALU.min))
                link(dve.scalar_tensor_tensor(sm(CANG), sm(ANG), -1.0, sm(ANG), ALU.mult, ALU.max))
                dve.tensor_scalar(sm(CANG), sm(CANG), -1.0, math.pi / 2, ALU.mult, ALU.add).then_inc(s.angles, 1)
                link(dve.tensor_tensor(sm(T1), lr, lr, ALU.mult))
                link(dve.tensor_tensor(sm(T2), li, li, ALU.mult))
                link(dve.tensor_tensor(sm(T1), sm(T1), sm(T2), ALU.add))
                link(dve.reciprocal(sm(RDEN), sm(T1)))

            def step_factor():
                dve.wait_ge(s.sines, 2)
                link(dve.tensor_tensor(t.pwr[:, 1, :], sm(MAG), sm(COS), ALU.mult))
                dve.tensor_tensor(t.pwi[:, 1, :], sm(MAG), sm(SIN), ALU.mult).then_inc(s.a_ready, 1)

            def input_factor():
                dve.wait_ge(s.a_ready, 1)
                ai = t.pwi[:, 1, :]
                link(dve.tensor_scalar(sm(T1), t.pwr[:, 1, :], -1.0, None, ALU.add))
                link(dve.tensor_tensor(sm(KR), sm(T1), lr, ALU.mult))
                link(dve.tensor_tensor(sm(T2), ai, li, ALU.mult))
                link(dve.tensor_tensor(sm(KR), sm(KR), sm(T2), ALU.add))
                link(dve.tensor_tensor(sm(KR), sm(KR), sm(RDEN), ALU.mult))
                link(dve.tensor_tensor(sm(KI), ai, lr, ALU.mult))
                link(dve.tensor_tensor(sm(T2), sm(T1), li, ALU.mult))
                link(dve.tensor_tensor(sm(KI), sm(KI), sm(T2), ALU.subtract))
                link(dve.tensor_tensor(sm(KI), sm(KI), sm(RDEN), ALU.mult))

            def discretise():
                dve.wait_ge(s.b_in, 2 * 2 * BLK * 16)
                dims = [P, PAIRS, GCH]
                kr, ki = (sm(k).unsqueeze(2).broadcast_to(dims) for k in (KR, KI))
                link(dve.tensor_tensor(tmp[:, 0], kr, t.Br[:], ALU.mult))
                link(dve.tensor_tensor(tmp[:, 1], ki, t.Bi[:], ALU.mult))
                link(dve.tensor_tensor(tmp[:, 2], kr, t.Bi[:], ALU.mult))
                link(dve.tensor_tensor(tmp[:, 3], ki, t.Br[:], ALU.mult))
                link(dve.tensor_tensor(t.Br[:], tmp[:, 0], tmp[:, 1], ALU.subtract))
                dve.tensor_tensor(t.Bi[:], tmp[:, 2], tmp[:, 3], ALU.add).then_inc(s.bbar, 1)
                dve.wait_ge(s.bbar, 1)

            def decay8():
                link(dve.tensor_tensor(sm(MAG8), sm(MAG), sm(MAG), ALU.mult))
                link(dve.tensor_tensor(sm(MAG8), sm(MAG8), sm(MAG8), ALU.mult))
                link(dve.tensor_tensor(sm(MAG8), sm(MAG8), sm(MAG8), ALU.mult))
                dve.wait_ge(s.d_in, 2 * BLK * 16)
                rows = slice(0, 2 * GCH)
                link(dve.tensor_tensor(t.patt[rows, :], t.ident[rows, 0:GCH], t.ident[rows, GCH:2 * GCH], ALU.add))
                diagonal(0)

            ssm_stages = (step_size, decay, angle, step_factor, input_factor, discretise, decay8)

            def diagonal(b):
                if b:
                    dve.wait_ge(s.km_done, b)
                else:
                    dve.wait_ge(s.bbar, 1)
                    dve.wait_ge(s.bd_zero, 1)
                pairs = slice(b * BP, (b + 1) * BP)
                for g in range(2):
                    h = slice(g * NST, (g + 1) * NST)
                    link(dve.tensor_copy(t.BDr[h, :, g, :], t.Br[h, pairs, :]))
                    last = dve.tensor_scalar(t.BDi[h, :, g, :], t.Bi[h, pairs, :], -1.0, None, ALU.mult)
                    if g == 0:
                        link(last)
                last.then_inc(s.bd_ready, 1)

            def scan_block(b):
                pairs = slice(b * BP, (b + 1) * BP)
                pr, pi = t.Pr[:, pairs, :], t.Pi[:, pairs, :]
                vr, vi = (banks[6][:, c * BP * NCH:(c + 1) * BP * NCH].rearrange("p (q k) -> p q k", k=NCH) for c in range(2))
                mag8 = t.sm[:, MAG8, pairs].unsqueeze(2).broadcast_to([P, BP, NCH - 1])
                if b == 0:
                    dve.wait_ge(s.turns, N_TURNS)
                    dve.wait_ge(s.zeros_ready, 1)
                link(dve.tensor_copy(t.M8[:, :, 1:NCH], mag8))
                dve.wait_ge(s.v_done, b + 1)
                link(dve.tensor_tensor(t.vr[:], vr, pr, ALU.mult))
                link(dve.tensor_tensor(t.ta[:], vi, pi, ALU.mult))
                link(dve.tensor_tensor(t.vr[:], t.vr[:], t.ta[:], ALU.add))
                link(dve.tensor_tensor(t.vi[:], vi, pr, ALU.mult))
                link(dve.tensor_tensor(t.ta[:], vr, pi, ALU.mult))
                link(dve.tensor_tensor(t.vi[:], t.vi[:], t.ta[:], ALU.subtract))

                def flat(a):
                    return a[:].rearrange("p q k -> p (q k)")

                link(dve.tensor_tensor_scan(flat(t.ta), flat(t.M8), flat(t.vr), 0.0, ALU.mult, ALU.add))
                link(dve.tensor_tensor_scan(flat(t.tb), flat(t.M8), flat(t.vi), 0.0, ALU.mult, ALU.add))
                link(dve.tensor_tensor(t.vr[:], t.ta[:], pr, ALU.mult))
                link(dve.tensor_tensor(t.vi[:], t.tb[:], pi, ALU.mult))
                if b:
                    dve.wait_ge(s.y_done, b)
                for g in range(2):
                    h = slice(g * NST, (g + 1) * NST)
                    link(dve.tensor_tensor(t.SBr[h, :, g, 1:NCH], t.vr[h, :, 0:NCH - 1], t.vi[h, :, 0:NCH - 1], ALU.subtract))
                link(dve.tensor_tensor(t.vr[:], t.tb[:], pr, ALU.mult))
                link(dve.tensor_tensor(t.vi[:], t.ta[:], pi, ALU.mult))
                h = slice(0, NST)
                link(dve.scalar_tensor_tensor(t.SBi[h, :, 0, 1:NCH], t.vr[h, :, 0:NCH - 1], -1.0, t.vi[h, :, 0:NCH - 1],
                                              ALU.mult, ALU.subtract))
                h = slice(NST, P)
                dve.scalar_tensor_tensor(t.SBi[h, :, 1, 1:NCH], t.vr[h, :, 0:NCH - 1], -1.0, t.vi[h, :, 0:NCH - 1],
                                         ALU.mult, ALU.subtract).then_inc(s.sb_ready, 1)

            dve.memset(t.cz[:, 0:2 * NCH], 0.0).then_inc(s.cz_zero, 1)

            for kind, i in STEPS:
                if (kind, i) in TILES:
                    idx = TILES.index((kind, i))
                    ps = banks[(idx + 2) % 3]
                    lo_pro(split_for((kind, i)))
                if kind == "split":
                    lo_pro(split_for(("v", 0)))
                elif kind == "X":
                    for h in range(2):
                        g = 2 * i + h
                        dve.wait_ge(s.rows_hi, g + 1)
                        hi, lo, c = (t.memT_hi, t.memT_lo, i) if i < MT else (t.xT_hi, t.xT_lo, i - MT)
                        at = (slice(None), slice(4 * h, 4 * h + 4), slice(c * P, (c + 1) * P))
                        dve.tensor_tensor(lo[at], banks[3 + g % 3][:, :].rearrange("p (k n) -> p k n", n=P), as_f32(hi[at]),
                                          ALU.subtract).then_inc(s.rows_lo, 1)
                elif kind == "dt":
                    dve.wait_ge(s.vec_in, 9 * 16)
                    rows = slice(LDT, LDT + PAIRS)
                    dve.tensor_copy(prm[rows, :].rearrange("p (g n) -> p g n", g=2),
                                    ldt[rows, :].unsqueeze(2).broadcast_to([PAIRS, 2, NST])).then_inc(s.dt_rows, 1)
                elif kind == "prm":
                    dve.wait_ge(s.vecs_T, 1)
                    dve.tensor_copy(t.prmT[:], banks[7][:, 0:N_VEC]).then_inc(s.vecs_cols, 1)
                elif kind == "C":
                    dve.wait_ge(s.c_T, 1)
                    dve.tensor_copy(t.CT[:].rearrange("p a q c -> p (a q c)"), banks[6][:, :]).then_inc(s.c_cols, 1)
                elif kind == "ssm":
                    ssm_stages[i]()
                elif kind in ("k", "v", "q"):
                    dve.wait_ge(s.pro_hi, SPLIT_TILES.index((kind, i)) + 1)
                    hi, lo, at, n = {"k": (t.kT_hi, t.kT_lo, i, M), "v": (t.v_hi, t.v_lo, i, CW),
                                     "q": (t.q_hi, t.q_lo, i % 2, S)}[kind]
                    dve.tensor_tensor(lo[:, at, :], ps[:, 0:n], as_f32(hi[:, at, :]), ALU.subtract).then_inc(s.bank_out, 1)
                elif kind == "S":
                    for b in range(2):
                        dve.wait_ge(s.scores_done, 2 * i + b + 1)
                        two = slice(2 * b, 2 * b + 2)
                        if i:
                            dve.wait_ge(s.exps_done, 4 * i)
                        link(dve.tensor_reduce(rmax[:, two], banks[3 + b][:, :].rearrange("p (a m) -> p a m", m=M),
                                               axis=AX.X, op=ALU.max))
                        dve.tensor_scalar(nmax[:, two], rmax[:, two], -SCALE, None, ALU.mult).then_inc(s.neg_max, 1)
                    dve.wait_ge(s.exps_done, 4 * i + 4)
                    link(dve.reciprocal(rinv, rsum))
                    for st in range(ST):
                        last = dve.tensor_scalar(t.probs[:, st, :], t.probs[:, st, :], rinv[:, st:st + 1], None, ALU.mult)
                        if st < ST - 1:
                            link(last)
                    last.then_inc(s.probs_norm, 1)
                elif kind == "T":
                    for mt in range(MT):
                        dve.wait_ge(s.pT_hi_ready, 2 * i + mt + 1)
                        dve.tensor_tensor(t.pT_lo[:, mt, :], banks[5 + mt][:, :], as_f32(t.pT_hi[:, mt, :]),
                                          ALU.subtract).then_inc(s.pT_lo_ready, 1)
                elif kind == "O":
                    dve.wait_ge(s.o_hi_ready, i + 1)
                    dve.tensor_tensor(t.o_lo[:, i, :], banks[7][:, :], as_f32(t.o_hi[:, i, :]), ALU.subtract).then_inc(s.o_lo_ready, 1)
                elif kind == "u":
                    if i < N_TILES["u"] - 1:
                        dve.wait_ge(s.part_done, parts_before((kind, i)))
                    else:
                        dve.wait_ge(s.w_used, units_after((kind, i)))
                    dve.tensor_copy(t.uN[:, :, 3 - i, :], ps[:, :].rearrange("p (g c) -> p g c", c=GCH)).then_inc(s.bank_out, 1)
                elif kind == "KM":
                    dve.wait_ge(s.km_done, i + 1)
                    if i:
                        dve.wait_ge(w3_in[i - 1], 2 * L * 16)
                    rows = slice(0, 2 * GCH)
                    ps = banks[5][rows, :].rearrange("p (q n) -> p q n", n=P)
                    dims = [2 * GCH, BP, GCH]
                    link(dve.tensor_tensor(t.DD[rows], t.Din[rows, i * BP:(i + 1) * BP].unsqueeze(2).broadcast_to(dims),
                                           t.patt[rows, :].unsqueeze(1).broadcast_to(dims), ALU.mult))
                    link(dve.tensor_tensor(t.Km[rows, :, 0:GCH], ps[:, :, 0:GCH], t.DD[rows], ALU.add))
                    dve.tensor_copy(t.Km[rows, :, GCH:P], ps[:, :, GCH:P]).then_inc(s.km_ready, 1)
                elif kind == "V":
                    scan_block(i)
                    if i + 1 < BLK:
                        diagonal(i + 1)
                elif kind == "YT":
                    dve.wait_ge(s.ys_hi_ready, i + 1)
                    dve.tensor_tensor(t.ys_lo[:, i, :], banks[5][:, :], as_f32(t.ys_hi[:, i, :]), ALU.subtract).then_inc(s.ys_lo_ready, 1)
                elif kind == "c":
                    ct, part, _ = conv_part(i)
                    dve.wait_ge(s.w_used, units_after((kind, i)))
                    tap = [t.prmT[:, CONVW + k * CT + ct:CONVW + k * CT + ct + 1] for k in range(3)]
                    if part == 0:
                        if ct == 0:
                            dve.wait_ge(s.o_done, HEADS)
                        else:
                            dve.wait_ge(s.z_lo_ready, ct)
                        dve.tensor_copy(t.cc[:], ps[:, :]).then_inc(s.bank_out, 1)
                        dve.wait_ge(s.bank_out, idx + 1)
                    elif part == 1:
                        if ct == 0:
                            dve.wait_ge(s.cz_zero, 1)
                        dve.tensor_tensor(t.cz[:, 2 * NCH:], ps[:, :], t.cc[:], ALU.mult).then_inc(s.bank_out, 1)
                        dve.wait_ge(s.bank_out, idx + 1)
                        link(dve.tensor_copy(t.cz[:, 0:2 * NCH].rearrange("p (j k) -> p j k", j=2)[:, :, 1:NCH],
                                             t.cz[:, S:S + 2 * NCH].rearrange("p (j k) -> p j k", j=2)[:, :, 0:NCH - 1]))
                        link(dve.tensor_scalar(t.cy[:], t.cz[:, 0:S], tap[0], None, ALU.mult))
                        link(dve.scalar_tensor_tensor(t.cy[:], t.cz[:, NCH:S + NCH], tap[1], t.cy[:], ALU.mult, ALU.add))
                        link(dve.scalar_tensor_tensor(t.cy[:], t.cz[:, 2 * NCH:], tap[2], t.cy[:], ALU.mult, ALU.add))
                    else:
                        dve.tensor_tensor(t.cc[:], ps[:, :], t.cy[:], ALU.mult).then_inc(s.bank_out, 1)
                        dve.wait_ge(s.bank_out, idx + 1)
                        dve.wait_ge(s.z_hi_ready, ct + 1)
                        dve.tensor_tensor(t.z_lo[:, ct, :], t.cc[:], as_f32(t.z_hi[:, ct, :]), ALU.subtract).then_inc(s.z_lo_ready, 1)
            lo_pro(N_PRO + RING)

            def merge_round(i, between=lambda: None):
                sg = t.sg
                m, v = t.mm[:, 0, :], t.mm[:, 1, :]

                def chain(k):
                    dve.wait_ge(s.merge_chain, i * 3 + k)

                dve.wait_ge(s.ya_done, i + 1)
                dve.wait_ge(s.gates_out, i * 4 + 1)
                dve.tensor_tensor(m, banks[3][:, :], sg[:, 0, :], ALU.mult).then_inc(s.bank_out, 1)
                dve.wait_ge(s.w_used, i * MIX_UNITS + (N_PRO + 4))
                dve.wait_ge(s.gates_out, i * 4 + 3)
                dve.tensor_tensor(v, banks[4][:, :], sg[:, 2, :], ALU.mult).then_inc(s.bank_out, 1)
                dve.wait_ge(s.bank_out, i * 3 + (len(TILES) + 2))
                dve.tensor_tensor(m, m, v, ALU.add).then_inc(s.merge_chain, 1)
                chain(1)
                between()
                dve.wait_ge(s.ga_done, i + 1)
                dve.tensor_tensor(v, banks[5][:, :], sg[:, 1, :], ALU.mult).then_inc(s.bank_out, 1)
                dve.wait_ge(s.bank_out, i * 3 + (len(TILES) + 3))
                dve.wait_ge(s.gates_out, i * 4 + 4)
                dve.tensor_tensor(v, v, sg[:, 3, :], ALU.mult).then_inc(s.merged, 1)
                dve.wait_ge(s.merged, i + 1)
                dve.tensor_tensor(m, m, v, ALU.add).then_inc(s.merge_chain, 1)
                chain(2)
                hi, lo = t.m_hi[:, bass.ds(i, 1), :], t.m_lo[:, bass.ds(i, 1), :]
                m3 = t.mm[:, 0:1, :]
                dve.tensor_copy(hi, m3).then_inc(s.merge_chain, 1)
                chain(3)
                dve.tensor_tensor(lo, m3, as_f32(hi), ALU.subtract).then_inc(s.m_lo_ready, 1)
                dve.wait_ge(s.m_lo_ready, i + 1)

            def lo_unit(slot, raw_slot, count):
                dve.wait_ge(s.w_hi_ready, count)
                hi, lo = split_slot(slot)
                dve.tensor_tensor(lo, t.raw[:, raw_slot, :], as_f32(hi), ALU.subtract).then_inc(s.w_lo_ready, 1)

            with dve.Fori(0, KD - 1) as i:
                for k in range(MIX_UNITS):
                    lo_unit(k, k, i * MIX_UNITS + (N_PRO + MIX_UNITS + k + 1))
                merge_round(i)
            for k in range(3):
                lo_unit(k, k, OUT0 + k + 1)
            merge_round(KD - 1, lambda: lo_unit(3, 3, OUT0 + 4))
            for k in range(4, RING2):
                lo_unit(k, k % RAW2, OUT0 + k + 1)

            def half_stats(st, h):
                dve.bn_stats(bn6[:, 6 * h:6 * h + 6], t.acc[:, st, h * S:(h + 1) * S]).then_inc(s.dve_stats, 1)

            def norm(n, st, gain, shift, dst, done):
                row = t.acc[:, st, :]
                dve.wait_ge(s.dve_stats, 2 * n + 2)
                link(dve.bn_aggr(mv, bn6))
                dve.tensor_scalar(ve, mv[:, 1:2], EPS, None, ALU.add).then_inc(s.var_ready, 1)
                link(dve.scalar_tensor_tensor(dst, row, mv[:, 0:1], gain[:], ALU.subtract, ALU.mult))
                dve.wait_ge(s.sd_ready, n + 1)
                link(dve.reciprocal(ry, sd))
                link(dve.scalar_tensor_tensor(rt, ry, ry, ve, ALU.mult, ALU.mult))
                link(dve.tensor_scalar(rt, rt, -0.5, 1.5, ALU.mult, ALU.add))
                link(dve.tensor_tensor(ry, ry, rt, ALU.mult))
                for h in range(2):
                    half = slice(h * S, (h + 1) * S)
                    dve.scalar_tensor_tensor(dst[:, half], dst[:, half], ry, shift[:, half], ALU.mult, ALU.add).then_inc(done, 1)

            def lo_x1(st):
                for h in range(2):
                    dve.wait_ge(s.x1T_hi, 2 * st + h + 1)
                    at = (slice(None), slice(4 * h, 4 * h + 4), slice(st * P, (st + 1) * P))
                    dve.tensor_tensor(t.xT_lo[at], banks[2 * st + h][:, :].rearrange("p (k n) -> p k n", n=P),
                                      as_f32(t.xT_hi[at]), ALU.subtract).then_inc(s.x1T_lo, 1)

            dve.wait_ge(s.acc_in, ST * 16)
            dve.wait_ge(s.vecs_in, 5 * 16)
            order = [(0, 0), (1, 0), (0, 1), (1, 1), (2, 0), (2, 1), (3, 0), (3, 1)]
            for n, (st, dh) in enumerate(order):
                if st < ST - 1:
                    dve.wait_ge(s.rows_done, n + 1)
                else:
                    dve.wait_ge(s.w_used, OUT0 + 4 * (dh + 1))
                row = t.acc[:, st, dh * S:(dh + 1) * S]
                dve.scalar_tensor_tensor(row, row, ALPHA, banks[2 * st + dh][:, :], ALU.mult, ALU.add).then_inc(s.rows_free, 1)
                if st >= 2:
                    dve.wait_ge(s.rows_free, n + 1)
                    half_stats(st, dh)
                if dh == 0:
                    continue
                if st < 2:
                    dve.wait_ge(s.rows_free, n + 1)
                    for h in range(2):
                        half_stats(st, h)
                if st >= 2:
                    dve.wait_ge(s.acc_ready, st - 1)
                    dve.wait_ge(s.x1_T, 2 * (st - 1))
                norm(st, st, t.ln1g, t.ln1b, x1_slot(st), s.x1_ready)
                if st == ST - 1:
                    lo_unit(2, 2, FF0 + 3)
                if st:
                    lo_x1(st - 1)
                if st == 2:
                    lo_unit(0, 0, FF0 + 1)
                    lo_unit(1, 1, FF0 + 2)
            lo_unit(3, 3, FF0 + 4)
            lo_x1(ST - 1)
            for k in range(4, 8):
                lo_unit(k, k % RAW2, FF0 + k + 1)

            dve.wait_ge(s.acc_ready, ST)

            def up_tiles(q):
                for r in range(FQ_TILES):
                    dve.wait_ge(s.sq_ready, q * FQ_TILES + (r + 1))
                    sq = t.sg[:, 2 + r % 2, :]
                    dve.tensor_copy(t.m_hi[:, r, :], sq).then_inc(s.h_hi_ready, 1)
                    dve.wait_ge(s.h_hi_ready, q * FQ_TILES + (r + 1))
                    dve.tensor_tensor(t.m_lo[:, r, :], sq, as_f32(t.m_hi[:, r, :]), ALU.subtract).then_inc(s.h_lo_ready, 1)
                    lo_unit(r, r % RAW2, q * FQ_UNITS + (FF0 + FQ_TILES + r + 1))

            def add_rows(q, step):
                st, dh = divmod(step, 2)
                if st < ST - 1:
                    dve.wait_ge(s.rows_done, q * 6 + (6 + step + 1))
                else:
                    dve.wait_ge(s.w_used, q * FQ_UNITS + (FF0 + FQ_TILES + 4 * (dh + 1)))
                row = t.acc[:, st, dh * S:(dh + 1) * S]
                dve.tensor_tensor(row, banks[step][:, :], row, ALU.add).then_inc(s.rows_free, 1)

            with dve.Fori(0, QUARTERS - 1) as q:
                up_tiles(q)
                for step in range(8):
                    add_rows(q, step)
                    if step >= 6:
                        for k in range(4):
                            u = 4 * (step - 6) + k
                            lo_unit(u, u % RAW2, q * FQ_UNITS + (FF0 + FQ_UNITS + u + 1))
            up_tiles(QUARTERS - 1)
            for st in range(ST):
                for dh in range(2):
                    add_rows(QUARTERS - 1, 2 * st + dh)
                    dve.wait_ge(s.rows_free, 8 * QUARTERS + 2 * st + dh + 1)
                    half_stats(st, dh)
                norm(ST + st, st, t.ln2g, t.ln2b, t.acc[:, st, :], s.y_ready)


def kernel(x, mem, w_in, b_gate, conv_w, w_conv_out, ssm_lam_re, ssm_lam_im, ssm_log_dt, ssm_b_re, ssm_b_im,
           ssm_c_re, ssm_c_im, ssm_d, w_glu, w_kv, w_xattn_out, w_out, ln1_g, ln1_b, w_up, b_up, w_down, b_down,
           ln2_g, ln2_b):
    import concourse.bacc as bacc
    from concourse.bass_utils import run_bass_kernel_spmd

    given = dict(x=x, mem=mem, w_in=w_in, b_gate=b_gate, conv_w=conv_w, w_conv_out=w_conv_out, lam_re=ssm_lam_re,
                 lam_im=ssm_lam_im, log_dt=ssm_log_dt, b_re=ssm_b_re, b_im=ssm_b_im, c_re=ssm_c_re, c_im=ssm_c_im,
                 ssm_d=ssm_d, w_glu=w_glu, w_kv=w_kv, w_xo=w_xattn_out, w_out=w_out, ln1_g=ln1_g, ln1_b=ln1_b,
                 w_up=w_up, b_up=b_up, w_down=w_down, b_down=b_down, ln2_g=ln2_g, ln2_b=ln2_b)
    nc = bacc.Bacc("TRN2", target_bir_lowering=False, num_devices=1)
    arrays, aps = {}, {}
    for name, value in given.items():
        arrays[f"in_{name}"] = np.ascontiguousarray(value)
        aps[name] = nc.dram_tensor(f"in_{name}", value.shape, F32, kind="ExternalInput").ap()
    out = nc.dram_tensor("out", x.shape, F32, kind="ExternalOutput").ap()
    build(nc, **aps, out=out)
    result = run_bass_kernel_spmd(nc, [arrays], core_ids=[0])
    return result.results[0]["out"]
```
